# Optimizing a Trainium2 kernel written in Bass

```python
import jax, jax.numpy as jnp
from jax import lax
import numpy as np

D_MODEL = 1024
BATCH = 1
SEQ = 1024
DEPTH = 1

CHUNK = 64
HEAD_DIM = 64
N_HEADS_SB = 8
N_HEADS_FOX = 8
D_SB = N_HEADS_SB * HEAD_DIM
D_FOX = N_HEADS_FOX * HEAD_DIM
D_FF = 4 * D_MODEL
Q_BLOCK = 128
N_IN = 3 * D_SB + 3 * D_FOX + N_HEADS_FOX
N_MOD = 6
EPS = 1e-6

kernel_name = "hybrid_stickbreak_forgetting_adaln_block"

def rmsnorm(x, g):
    xf = x.astype(jnp.float32)
    y = xf * lax.rsqrt(jnp.mean(xf * xf, axis=-1, keepdims=True) + EPS)
    return (y * g.astype(jnp.float32)).astype(x.dtype)

def modulate(h, shift, scale):
    return h * (1.0 + scale[:, None, :]) + shift[:, None, :]

def to_heads(t, n_heads):
    b, s, _ = t.shape
    return t.reshape(b, s, n_heads, HEAD_DIM).transpose(0, 2, 1, 3)

def to_query_blocks(t):
    b, h, s, d = t.shape
    return t.reshape(b, h, s // Q_BLOCK, Q_BLOCK, d).transpose(2, 0, 1, 3, 4)

def from_query_blocks(o):
    nblk, b, h, qb, d = o.shape
    return o.transpose(1, 0, 3, 2, 4).reshape(b, nblk * qb, h * d)

def stick_breaking_attention(q, k, v):
    s_len = q.shape[2]
    scale = HEAD_DIM ** -0.5
    kf = k.astype(jnp.float32)
    vf = v.astype(jnp.float32)
    key_pos = jnp.arange(s_len)

    def block(args):
        qb, i = args
        q_pos = i * Q_BLOCK + jnp.arange(Q_BLOCK)
        z = jnp.einsum('bhqd,bhkd->bhqk', qb.astype(jnp.float32), kf) * scale
        valid = key_pos[None, :] < q_pos[:, None]
        log_1m_beta = jnp.where(valid, jax.nn.log_sigmoid(-z), 0.0)
        suffix = lax.cumsum(log_1m_beta, axis=3, reverse=True) - log_1m_beta
        w = jnp.where(valid, jnp.exp(jax.nn.log_sigmoid(z) + suffix), 0.0)
        return jnp.einsum('bhqk,bhkd->bhqd', w, vf)

    out = lax.map(block, (to_query_blocks(q), jnp.arange(s_len // Q_BLOCK)))
    return from_query_blocks(out)

def forgetting_attention(q, k, v, log_f):
    b, h, s_len, _ = q.shape
    scale = HEAD_DIM ** -0.5
    kf = k.astype(jnp.float32)
    vf = v.astype(jnp.float32)
    F = jnp.cumsum(log_f.astype(jnp.float32), axis=-1)
    F_blocks = F.reshape(b, h, s_len // Q_BLOCK, Q_BLOCK).transpose(2, 0, 1, 3)
    key_pos = jnp.arange(s_len)

    def block(args):
        qb, Fq, i = args
        q_pos = i * Q_BLOCK + jnp.arange(Q_BLOCK)
        z = jnp.einsum('bhqd,bhkd->bhqk', qb.astype(jnp.float32), kf) * scale
        z = z + Fq[..., :, None] - F[:, :, None, :]
        valid = key_pos[None, :] <= q_pos[:, None]
        p = jax.nn.softmax(jnp.where(valid, z, -jnp.inf), axis=-1)
        return jnp.einsum('bhqk,bhkd->bhqd', p, vf)

    out = lax.map(block, (to_query_blocks(q), F_blocks, jnp.arange(s_len // Q_BLOCK)))
    return from_query_blocks(out)

def setup_inputs(seed: int = 0) -> dict:
    key = jax.random.key(seed)
    ks = jax.random.split(key, 20)
    f32 = jnp.float32
    nrm = lambda k, shape, s: (jax.random.normal(k, shape, f32) * s)
    D = D_MODEL
    return {
        "x": nrm(ks[0], (BATCH, SEQ, D), 1.0),
        "c": nrm(ks[1], (BATCH, D), 1.0),
        "w_ada": nrm(ks[2], (DEPTH, D, N_MOD * D), 0.2 * D ** -0.5),
        "b_ada": nrm(ks[3], (DEPTH, N_MOD * D), 0.02),
        "g_mix": 1.0 + nrm(ks[4], (DEPTH, D), 0.02),
        "w_in": nrm(ks[5], (DEPTH, D, N_IN), D ** -0.5),
        "b_f": 3.0 + nrm(ks[6], (DEPTH, N_HEADS_FOX), 0.5),
        "w_gate": nrm(ks[7], (DEPTH, D, 2 * D), D ** -0.5),
        "b_gate": nrm(ks[8], (DEPTH, 2 * D), 0.02),
        "w_out_sb": nrm(ks[9], (DEPTH, D_SB, D), D_SB ** -0.5),
        "w_out_fox": nrm(ks[10], (DEPTH, D_FOX, D), D_FOX ** -0.5),
        "w_o": nrm(ks[11], (DEPTH, D, D), D ** -0.5),
        "g_mlp": 1.0 + nrm(ks[12], (DEPTH, D), 0.02),
        "w_ff1": nrm(ks[13], (DEPTH, D, D_FF), D ** -0.5),
        "b_ff1": nrm(ks[14], (DEPTH, D_FF), 0.02),
        "w_ff2": nrm(ks[15], (DEPTH, D_FF, D), D_FF ** -0.5),
        "b_ff2": nrm(ks[16], (DEPTH, D), 0.02),
        "g_final": 1.0 + nrm(ks[17], (D,), 0.02),
    }

def reference(x, c, w_ada, b_ada, g_mix, w_in, b_f, w_gate, b_gate, w_out_sb, w_out_fox,
              w_o, g_mlp, w_ff1, b_ff1, w_ff2, b_ff2, g_final):
    o_qkv_sb = 3 * D_SB
    o_qkv_fox = o_qkv_sb + 3 * D_FOX
    for layer in range(DEPTH):
        mod = c @ w_ada[layer] + b_ada[layer]
        sh1, sc1, gt1, sh2, sc2, gt2 = jnp.split(mod, N_MOD, axis=-1)

        h = modulate(rmsnorm(x, g_mix[layer]), sh1, sc1)
        proj = h @ w_in[layer]
        q_sb, k_sb, v_sb = jnp.split(proj[..., :o_qkv_sb], 3, axis=-1)
        q_fx, k_fx, v_fx = jnp.split(proj[..., o_qkv_sb:o_qkv_fox], 3, axis=-1)
        log_f = jax.nn.log_sigmoid(proj[..., o_qkv_fox:].astype(jnp.float32)
                                   + b_f[layer]).transpose(0, 2, 1)

        o_sb = stick_breaking_attention(to_heads(q_sb, N_HEADS_SB), to_heads(k_sb, N_HEADS_SB),
                                        to_heads(v_sb, N_HEADS_SB)).astype(x.dtype)
        o_fx = forgetting_attention(to_heads(q_fx, N_HEADS_FOX), to_heads(k_fx, N_HEADS_FOX),
                                    to_heads(v_fx, N_HEADS_FOX), log_f).astype(x.dtype)

        gates = jax.nn.sigmoid(h @ w_gate[layer] + b_gate[layer])
        g_sb, g_fx = jnp.split(gates, 2, axis=-1)
        merged = g_sb * (o_sb @ w_out_sb[layer]) + g_fx * (o_fx @ w_out_fox[layer])
        x = x + gt1[:, None, :] * (merged @ w_o[layer])

        h = modulate(rmsnorm(x, g_mlp[layer]), sh2, sc2)
        u = jnp.square(jax.nn.relu(h @ w_ff1[layer] + b_ff1[layer]))
        x = x + gt2[:, None, :] * (u @ w_ff2[layer] + b_ff2[layer])

    return rmsnorm(x, g_final)


_drawn_inputs = setup_inputs


def setup_inputs(seed=0):
    import zlib

    import numpy as np

    out = dict(_drawn_inputs(seed))
    spreads = {}
    factors = {'g_mix': 8.0,
     'b_f': 5.929,
     'b_gate': 21.994,
     'g_mlp': 8.0,
     'b_ff1': 8.0,
     'b_ff2': 200.0,
     'g_final': 24.266}
    for name, (base, spread) in spreads.items():
        noise = np.random.default_rng([zlib.crc32(name.encode()), seed]).standard_normal(out[name].shape)
        drawn = base * np.exp(spread * noise) if base else spread * noise
        out[name] = __import__('jax').numpy.asarray(drawn.astype(out[name].dtype))
    for name, factor in factors.items():
        out[name] = (out[name] * factor).astype(out[name].dtype)
    return out
```

```python
from contextlib import ExitStack

import concourse.bass as bass
from concourse import mybir

P = 128
D = 1024
T = 1024
KT = D // P
HALF = 512
HEADS = 8
DH = 64
D_MIX = HEADS * DH
D_FF = 4 * D
N_MOD = 6
QB = T // P
PAIRS = HEADS // 2
UNITS = 2 * QB
EPS = 1e-6
SCALE = DH ** -0.5
NEG = -1.0e30
FF_CHUNKS = 4

F32 = mybir.dt.float32
F32R = mybir.dt.float32r
BF16 = mybir.dt.bfloat16
ALU = mybir.AluOpType
ACT = mybir.ActivationFunctionType
AX = mybir.AxisListType

COL_GMIX, COL_GMLP, COL_BGATE, COL_BFF1, COL_C, COL_GFIN, COL_BFF2, COL_BADA = 0, 8, 16, 32, 64, 72, 80, 88
PACK1 = COL_BADA
PACK2 = N_MOD * KT

DONE_F, DONE_ITER = 2, 6
DONE_MERGE = DONE_F + 2 * PAIRS * DONE_ITER
DONE_WO = DONE_MERGE + 4 * KT
DONE_FF = DONE_WO + 2 * KT
FREE_F, FREE_ITER = 2, 4
FREE_MERGE = FREE_F + 2 * PAIRS * FREE_ITER
FREE_WO = FREE_MERGE + 2 * KT
FREE_FF = FREE_WO + 2 * KT
START = 1
USE_MERGE = (1 + 3 * 2 * PAIRS, 2 * 2 * PAIRS)
USE_WO = (USE_MERGE[0] + KT // 2, USE_MERGE[1] + KT // 2)
USE_FF = (USE_WO[0] + KT // 2, USE_WO[1] + KT // 2)
V_CHUNKS = 2


def chunks_of(u):
    first = V_CHUNKS
    for w in range(u):
        first += 1 if w % QB < 4 else 2
    return list(range(first, first + (1 if u % QB < 4 else 2)))


TP_ITER = chunks_of(UNITS - 1)[-1] + 1
GATE_LAG = 1
STEPS = UNITS + 3


def build_block(nc, x, c, w_ada, b_ada, g_mix, w_in, b_f, w_gate, b_gate, w_out_sb, w_out_fox,
                w_o, g_mlp, w_ff1, b_ff1, w_ff2, b_ff2, g_final, out):
    x_rows = x.rearrange("b (t p) d -> (b t) p d", p=P)
    out_rows = out.rearrange("b (t p) d -> (b t) p d", p=P)
    tiles_of = lambda w: w.rearrange("l (k p) n -> p (l k) n", p=P)
    ada_t, in_t, gate_t, wo_t, ff1_t = map(tiles_of, (w_ada, w_in, w_gate, w_o, w_ff1))
    osb_t, ofx_t, ff2_t = map(tiles_of, (w_out_sb, w_out_fox, w_ff2))
    rows_of = lambda v: v.rearrange("l (r q) -> (l r) q", q=P)
    xT_dram = nc.dram_tensor("xT_dram", [KT, P, T], F32, kind="Internal").ap()
    gates_dram = nc.dram_tensor("gates_dram", [2 * KT, P, T], F32, kind="Internal").ap()
    fparts_dram = nc.dram_tensor("fparts_dram", [HEADS, 3, T], BF16, kind="Internal").ap()

    base = (nc.sbuf_base + 31) // 32 * 32
    KB = 1024
    R1, R2, R3, R4, R5, R6 = (base + n * KB for n in (0, 64, 128, 160, 184, 196))
    R7 = base + 204 * KB

    def at(name, offset, shape, dtype):
        return nc.alloc_sbuf_tensor_at(name, shape, dtype, offset=offset)

    h1 = [at(f"h1_{s}", R1 + n * 32 * KB, [P, KT, T], F32R) for n, s in enumerate(("hi", "lo"))]
    o_split = [at(f"o_{s}", R1 + n * 32 * KB, [P, KT, T], F32R) for n, s in enumerate(("hi", "lo"))]
    h2 = [at(f"h2_{s}", R1 + n * 32 * KB, [P, KT, T], F32R) for n, s in enumerate(("hi", "lo"))]
    x_in = at("x_in", R2, [P, KT, T], F32)
    sq_a = at("sq_a", R2 + 32 * KB, [P, 2, HALF], F32)
    ss_a = at("ss_a", R2 + 36 * KB, [P, T], F32)
    rstd_a = at("rstd_a", R2 + 40 * KB, [P, T], F32)
    norm_a = at("norm_a", R2 + 44 * KB, [P, 2, HALF], F32)
    pack1 = at("pack1", R2 + 48 * KB, [PACK1, P], F32)
    pack2 = at("pack2", R2 + 49 * KB, [PACK2, P], F32)
    q_hi = [at(f"q_hi{h}", R2 + 4 * h * KB, [P, T], F32R) for h in range(2)]
    q_lo = [at(f"q_lo{h}", R2 + (8 + 4 * h) * KB, [P, T], F32R) for h in range(2)]
    k_st = [at(f"k_st{h}", R2 + (16 + 4 * h) * KB, [P, T], F32R) for h in range(2)]
    v_st = at("v_st", R2 + 24 * KB, [P, QB, 2, 2, DH], F32R)
    prob = at("prob", R2 + 32 * KB, [P, 2, T], F32)
    surv = at("surv", R2 + 40 * KB, [P, 2, T], F32)
    wT = [at(f"wT_{s}", R2 + (48 + 8 * n) * KB, [P, QB, 2 * P], F32R) for n, s in enumerate(("hi", "lo"))]
    f_abs = at("f_abs", R2 + 40 * KB, [HEADS, T], F32)
    f_log = at("f_log", R2 + 44 * KB, [HEADS, T], F32)
    f_cum = at("f_cum", R2 + 48 * KB, [HEADS, T], F32)
    f_rest = at("f_rest", R2 + 52 * KB, [HEADS, T], F32)
    f_parts = at("f_parts", R2 + 56 * KB, [HEADS, 3, T], BF16)
    merged = [at(f"merged_{s}", R2 + n * 32 * KB, [P, KT, T], F32R) for n, s in enumerate(("hi", "lo"))]
    hid = [at(f"hid_{s}", R2 + n * 32 * KB, [P, KT, T], F32R) for n, s in enumerate(("hi", "lo"))]
    out_st = at("out_st", R2, [P, 2, T], F32)
    xT = at("xT", R3, [P, KT, T], F32)
    mixed = at("mixed", R3, [P, KT, T], F32)
    res = at("res", R3, [P, KT, T], F32)
    w_raw = [at(f"w_raw{b}", R4 + 4 * b * KB, [P, KT, P], F32) for b in range(2)]
    w_hi = [at(f"w_hi{b}", R4 + (8 + 4 * b) * KB, [P, KT, P], F32R) for b in range(2)]
    w_lo = [at(f"w_lo{b}", R4 + (16 + 4 * b) * KB, [P, KT, P], F32R) for b in range(2)]
    ada = at("ada", R5, [P, 2, D], F32)
    ada_sum = at("ada_sum", R5 + 8 * KB, [P, D], F32)
    q_f = [at(f"q_f{h}", R5 + 4 * h * KB, [6, T], BF16) for h in range(2)]
    k_f = [at(f"k_f{h}", R5 + (4 * h + 2) * KB, [6, T], BF16) for h in range(2)]
    gates = at("gates", R5, [P, 2, 2, HALF], F32)
    ss_b = at("ss_b", R5, [P, T], F32)
    rstd_b = at("rstd_b", R5 + 4 * KB, [P, T], F32)
    sq_b = at("sq_b", R5 + 8 * KB, [P, 2, HALF], F32)
    gate_st = at("gate_st", R6, [P, 2, HALF], F32)
    vT = at("vT", R6, [P, T], F32)
    fold = at("fold", R6 + 4 * KB, [P, 2 * P], F32)
    x_again = at("x_again", R6, [P, 2, HALF], F32)
    norm_b = at("norm_b", R6 + 4 * KB, [P, 2, HALF], F32)
    relu = at("relu", R6, [P, 2, HALF], F32)
    relu_sq = at("relu_sq", R6 + 4 * KB, [P, 2, HALF], F32)
    spot = [R7]

    def small(name, shape, dtype):
        n = 1
        for s in shape[1:]:
            n *= s
        t = at(name, spot[0], shape, dtype)
        spot[0] += (n * (2 if dtype == BF16 else 4) + 31) // 32 * 32
        assert spot[0] <= nc.sbuf_usable_end
        return t

    ident = small("ident", [P, P], F32)
    ones = small("ones", [P, P], F32)
    ident_b = small("ident_b", [P, P], BF16)
    mask_b = [small(f"mask_b{m}", [P, P], BF16) for m in range(2)]
    cols = small("cols", [P, PACK1 + PACK2], F32)
    mod = small("mod", [P, N_MOD * KT], F32)
    g_sc = [small(f"g_sc{n}", [P, KT], F32) for n in range(2)]
    gt_b = small("gt_b", [P, KT], F32)
    eps_col = small("eps_col", [P, 1], F32)
    bf_col = small("bf_col", [HEADS, 1], F32)
    neg_max = small("neg_max", [P, 2], F32)
    row_sum = small("row_sum", [P, 2], F32)
    inv_sum = small("inv_sum", [P, 2], F32)

    with ExitStack() as ctx:
        ps = ctx.enter_context(nc.psum_tensor("ps", [P, 8, HALF], F32))
        scores = [ps[:, 2 * s:2 * s + 2, :].rearrange("p a b -> p (a b)") for s in range(2)]
        sem = lambda name: ctx.enter_context(nc.semaphore(name))

        consts_made = sem("consts_made")
        identity_made = sem("identity_made")
        small_loaded = sem("small_loaded")
        x_loaded = sem("x_loaded")
        pack_turned, cols_made = sem("pack_turned"), sem("cols_made")
        ada_loaded = [sem(f"ada_loaded{b}") for b in range(2)]
        ada_used, ada_summed, mod_made, mod_derived = (sem(n) for n in ("ada_used", "ada_summed", "mod_made", "mod_derived"))
        x_turned, x_kept_act, x_kept_dve, x_saved = (sem(n) for n in ("x_turned", "x_kept_act", "x_kept_dve", "x_saved"))
        squared, sq_summed, stats_done, root_done, rstd_made = (
            sem(n) for n in ("squared", "sq_summed", "stats_done", "root_done", "rstd_made"))
        normed, h_hi, h_ready = sem("normed"), sem("h_hi"), sem("h_ready")
        w_loaded = [sem(f"w_loaded{b}") for b in range(2)]
        hi_split = [sem(f"hi_split{b}") for b in range(2)]
        w_split = [sem(f"w_split{b}") for b in range(2)]
        dense_done, dense_free = sem("dense_done"), sem("dense_free")
        f_step_dve, f_step_act, f_stored, f_loaded, f_ones = (
            sem(n) for n in ("f_step_dve", "f_step_act", "f_stored", "f_loaded", "f_ones"))
        v_copied, k_hi_done, q_hi_done = sem("v_copied"), sem("k_hi_done"), sem("q_hi_done")
        scores_ready, scores_used = sem("scores_ready"), sem("scores_used")
        scanned, max_ready, inv_ready, probs_ready = (sem(n) for n in ("scanned", "max_ready", "inv_ready", "probs_ready"))
        tp_done, tp_hi, tp_free = sem("tp_done"), sem("tp_hi"), sem("tp_free")
        av_done, av_folded, av_free = sem("av_done"), sem("av_folded"), sem("av_free")
        gate_done, gate_copied = sem("gate_done"), sem("gate_copied")
        gate_saved = [sem(f"gate_saved{b}") for b in range(2)]
        gate_back = [sem(f"gate_back{b}") for b in range(2)]
        o_hi_done, o_ready = sem("o_hi_done"), sem("o_ready")
        gate_on, merge_mul, merge_sum, merge_hi = (sem(n) for n in ("gate_on", "merge_mul", "merge_sum", "merge_hi"))
        x_back = [sem(f"x_back{b}") for b in range(2)]
        act_free, hid_hi, relu_squared, hid_ready = (sem(n) for n in ("act_free", "hid_hi", "relu_squared", "hid_ready"))
        y_ready, y_turned, y_copied_act, y_copied_dve = (sem(n) for n in ("y_ready", "y_turned", "y_copied_act", "y_copied_dve"))
        out_saved = [sem(f"out_saved{b}") for b in range(2)]

        block = ctx.enter_context(nc.Block())

        @block.sync
        def _(sp):
            for r, v in ((COL_GMIX, g_mix), (COL_GMLP, g_mlp), (COL_BGATE, b_gate), (COL_BFF1, b_ff1),
                         (COL_C, c), (COL_GFIN, g_final.rearrange("(l d) -> l d", l=1)), (COL_BFF2, b_ff2)):
                src = rows_of(v)
                sp.dma_start(pack1[r:r + src.shape[0], :], src).then_inc(small_loaded, 16)
            sp.dma_start(pack2[:, :], rows_of(b_ada)).then_inc(small_loaded, 16)
            sp.dma_start(bf_col[:, :], b_f.rearrange("l h -> h l")).then_inc(small_loaded, 16)
            for t in range(KT):
                sp.dma_start(x_in[:, t, :], x_rows[t]).then_inc(x_loaded, 16)

            def load_ada(m, k, first=False):
                if not first:
                    sp.wait_ge(ada_used, KT * m + k - 1)
                sp.dma_start(ada[:, k % 2, :], ada_t[:, k, bass.ds(D * m, D)]).then_inc(ada_loaded[k % 2], 16)

            def load_w(b, use, parts, first=False):
                if not first:
                    sp.wait_ge(w_split[b], START + 2 * use)
                for hf in (1, 0):
                    src = parts[hf]
                    sp.dma_start(w_raw[b][:, 4 * hf:4 * hf + 4, 0:src.shape[2]], src).then_inc(w_loaded[b], 16)

            halves = lambda w, col, n=P: [w[:, 0:4, bass.ds(col, n)], w[:, 4:8, bass.ds(col, n)]]

            for k in range(KT):
                load_ada(0, k, first=k < 2)
            load_w(0, 0, halves(in_t, 6 * D_MIX, HEADS), first=True)
            for k in range(KT):
                load_ada(1, k)
            sp.wait_ge(x_kept_act, KT)
            sp.wait_ge(x_kept_dve, KT)
            sp.dma_start(xT_dram.rearrange("k p t -> p k t"), xT[:, :, :]).then_inc(x_saved, 16)

            def pair_loads(G, k_col, q_col, v_col, fox):
                load_w(0, 3 * G + 1, halves(in_t, k_col))
                if not fox:
                    load_ada(G + 2, 0)
                    load_ada(G + 2, 1)
                load_w(1, 2 * G, halves(in_t, q_col))
                if not fox:
                    load_ada(G + 2, 2)
                    load_ada(G + 2, 3)
                else:
                    sp.wait_ge(scores_ready, UNITS * G)
                    for h in range(2):
                        src = fparts_dram[bass.ds(2 * (G - PAIRS) + h, 1)].rearrange("a r t -> (a r) t")
                        sp.dma_start(q_f[h][0:3, :], src).then_inc(f_loaded, 16)
                        sp.dma_start(k_f[h][3:6, :], src).then_inc(f_loaded, 16)
                load_w(0, 3 * G + 2, halves(in_t, v_col))
                if not fox:
                    load_ada(G + 2, 4)
                    load_ada(G + 2, 5)
                load_w(1, 2 * G + 1, halves(gate_t, 2 * P * G))
                if not fox:
                    load_ada(G + 2, 6)
                    load_ada(G + 2, 7)
                load_w(0, 3 * G + 3, halves(gate_t, 2 * P * G + P))

            with sp.Fori(0, PAIRS) as G:
                pair_loads(G, D_MIX + P * G, P * G, 2 * D_MIX + P * G, False)
            sp.wait_ge(f_stored, 16)
            sp.wait_ge(f_ones, 4)
            with sp.Fori(PAIRS, 2 * PAIRS) as G:
                at_g = 3 * D_MIX - P * PAIRS + P * G
                pair_loads(G, at_g + D_MIX, at_g, at_g + 2 * D_MIX, True)
            for n in range(KT):
                load_w(n % 2, USE_MERGE[n % 2] + n // 2, [osb_t[:, :, P * n:P * n + P], ofx_t[:, :, P * n:P * n + P]])
            with sp.Fori(0, KT // 2) as n:
                for b in range(2):
                    load_w(b, USE_WO[b] + n, halves(wo_t, 2 * P * n + P * b))
            with sp.Fori(0, FF_CHUNKS) as ch:
                with sp.Fori(0, KT // 2) as n:
                    for b in range(2):
                        load_w(b, USE_FF[b] + KT * ch + n, halves(ff1_t, D * ch + 2 * P * n + P * b))
                with sp.Fori(0, KT // 2) as n:
                    for b in range(2):
                        col = 2 * P * n + P * b
                        load_w(b, USE_FF[b] + KT * ch + KT // 2 + n,
                               [ff2_t[:, bass.ds(KT * ch + 4 * hf, 4), bass.ds(col, P)] for hf in range(2)])
            for t in range(QB):
                sp.wait_ge(y_copied_act, t + 1)
                sp.wait_ge(y_copied_dve, t + 1)
                sp.dma_start(out_rows[t], out_st[:, t % 2, :]).then_inc(out_saved[t % 2], 16)
            for b in range(2):
                sp.wait_ge(out_saved[b], 16 * QB // 2)

        @block.gpsimd
        def _(pool):
            for b in range(2):
                pool.sem_inc(w_split[b], START)
            nc.gpsimd.memset(ident[:, :], 0.0).then_inc(identity_made, 1)
            nc.gpsimd.memset(ident_b[:, :], 0.0).then_inc(identity_made, 1)
            for m in range(2):
                nc.gpsimd.memset(mask_b[m][:, :], 0.0).then_inc(identity_made, 1)
            nc.gpsimd.memset(ones[:, :], 1.0).then_inc(consts_made, 1)
            nc.gpsimd.memset(eps_col[:, :], EPS).then_inc(consts_made, 1)
            pool.wait_ge(identity_made, 4)
            for t in (ident, ident_b):
                nc.gpsimd.affine_select(out=t[:, :], in_=t[:, :], compare_op=ALU.not_equal, fill=1.0, base=0,
                                        pattern=[[-1, P]], channel_multiplier=1).then_inc(consts_made, 1)
            for m, op in enumerate((ALU.is_gt, ALU.is_ge)):
                nc.gpsimd.affine_select(out=mask_b[m][:, :], in_=mask_b[m][:, :], compare_op=op, fill=NEG, base=0,
                                        pattern=[[-1, P]], channel_multiplier=1).then_inc(consts_made, 1)

            def split(b, use, n=P):
                one = ones[:, 0:n].unsqueeze(1).broadcast_to([P, 4, n])
                pool.wait_ge(w_loaded[b], 32 * use + 32)
                for hf in range(2):
                    raw = w_raw[b][:, 4 * hf:4 * hf + 4, 0:n]
                    hi = w_hi[b][:, 4 * hf:4 * hf + 4, 0:n]
                    lo = w_lo[b][:, 4 * hf:4 * hf + 4, 0:n]
                    nc.gpsimd.tensor_tensor(hi, raw, one, ALU.mult).then_inc(hi_split[b], 1)
                    pool.wait_ge(hi_split[b], 2 * use + hf + 1)
                    nc.gpsimd.tensor_tensor(lo, raw, hi.bitcast(F32), ALU.subtract).then_inc(w_split[b], 1)

            split(0, 0, HEADS)
            with pool.Fori(0, 2 * PAIRS) as G:
                done = DONE_F + DONE_ITER * G
                pool.wait_ge(gate_done, START + 4 * G)
                pool.wait_ge(dense_done, done)
                split(0, 3 * G + 1)
                split(1, 2 * G)
                pool.wait_ge(dense_done, done + 2)
                split(0, 3 * G + 2)
                pool.wait_ge(dense_done, done + 4)
                split(1, 2 * G + 1)
                pool.wait_ge(dense_done, done + 6)
                split(0, 3 * G + 3)
            pool.wait_ge(gate_done, START + 8 * PAIRS)
            with pool.Fori(0, KT // 2) as n:
                for b in range(2):
                    pool.wait_ge(dense_done, DONE_MERGE - 4 + 4 * (2 * n + b))
                    split(b, USE_MERGE[b] + n)
            with pool.Fori(0, KT // 2) as n:
                for b in range(2):
                    pool.wait_ge(dense_done, DONE_WO - 2 + 2 * (2 * n + b))
                    split(b, USE_WO[b] + n)
            with pool.Fori(0, FF_CHUNKS * KT) as n:
                for b in range(2):
                    pool.wait_ge(dense_done, DONE_FF - 2 + 2 * (2 * n + b))
                    split(b, USE_FF[b] + n)

        @block.tensor
        def _(pe):
            pe.sem_inc(gate_done, START)
            pe.sem_inc(av_done, START)
            def three(dst, b, k, rhs, cols_, start, stop, m=P):
                pe.matmul(dst, w_hi[b][:, k, 0:m], rhs[0][:, k, cols_], start=start, stop=False)
                pe.matmul(dst, w_hi[b][:, k, 0:m], rhs[1][:, k, cols_], start=False, stop=False)
                return pe.matmul(dst, w_lo[b][:, k, 0:m], rhs[0][:, k, cols_], start=False, stop=stop)

            halves = [slice(0, HALF), slice(HALF, T)]

            def dense(b, use, rhs, bank, m=P, ready=None):
                for k in range(KT):
                    if k % 4 == 0:
                        pe.wait_ge(w_split[b], START + 2 * use + k // 4 + 1)
                    if ready is not None:
                        pe.wait_ge(*ready(k))
                    for hf in range(2):
                        mm = three(ps[0:m, bank + hf, :], b, k, rhs, halves[hf], k == 0, k == KT - 1, m)
                        if k == KT - 1:
                            mm.then_inc(dense_done, 1)

            def norm_stats(which, ss):
                pe.wait_ge(sq_summed, 2 * KT * (which + 1))
                for hf in range(2):
                    mm = pe.matmul(ps[:, 4 + hf, :], ones[:, :], ss[:, halves[hf]], start=True, stop=True)
                mm.then_inc(stats_done, 1)

            def ada_total(m):
                pe.wait_ge(ada_used, KT * (m + 1))
                for n in range(KT):
                    mm = pe.matmul(ps[:, 6, n:n + 1], ada_sum[:, P * n:P * n + P], ones[:, 0:1], start=True, stop=True)
                mm.then_inc(ada_summed, 1)

            pe.wait_ge(consts_made, 6)
            pe.wait_ge(small_loaded, 16 * 9)
            pe.transpose(ps[:, 6, 0:PACK1], pack1[:, :], ident[0:PACK1, 0:PACK1])
            pe.transpose(ps[:, 6, PACK1:PACK1 + PACK2], pack2[:, :], ident[0:PACK2, 0:PACK2]).then_inc(pack_turned, 1)
            pe.wait_ge(x_loaded, 16 * KT)
            for k in range(KT):
                if k >= 2:
                    pe.wait_ge(x_kept_act, k - 1)
                    pe.wait_ge(x_kept_dve, k - 1)
                for t in range(QB):
                    mm = pe.transpose(ps[:, 2 * (k % 2) + t // 4, P * (t % 4):P * (t % 4) + P],
                                      x_in[:, t, P * k:P * k + P], ident[:, :])
                    if t % 4 == 3:
                        mm.then_inc(x_turned, 1)
            norm_stats(0, ss_a)
            pe.wait_ge(cols_made, 1)
            ada_total(0)
            pe.wait_ge(mod_made, 1)
            ada_total(1)
            dense(0, 0, h1, 2, m=HEADS, ready=lambda k: (h_ready, 2 * k + 2))

            def attend(G, fox):
                pe.wait_ge(scores_used, START + UNITS * G)
                dense(0, 3 * G + 1, h1, 0)
                pe.wait_ge(dense_free, FREE_F + FREE_ITER * G)
                dense(1, 2 * G, h1, 2)
                pe.wait_ge(av_free, START + QB * G)
                pe.wait_ge(gate_copied, START + 4 * G)
                pe.wait_ge(mod_made, 2)
                dense(0, 3 * G + 2, h1, 6)

                def turn(idx, blocks, src):
                    if idx == 0:
                        pe.wait_ge(tp_free, START + TP_ITER * G)
                    else:
                        pe.wait_ge(tp_free, START + TP_ITER * G + idx - 1)
                    for n, blk in enumerate(blocks):
                        mm = pe.transpose(ps[:, 4 + idx % 2, P * n:P * n + P], src[:, P * blk:P * blk + P], ident[:, :])
                    mm.then_inc(tp_done, 1)

                def turn_values():
                    pe.wait_ge(v_copied, 2 * G + 2)
                    for idx in range(V_CHUNKS):
                        turn(idx, range(4 * idx, 4 * idx + 4), vT)
                    if not fox:
                        ada_total(G + 2)

                def score(u):
                    h, i = divmod(u, QB)
                    if u < 2:
                        pe.wait_ge(dense_free, FREE_F + FREE_ITER * (G + 1))
                        if fox and u == 0:
                            pe.wait_ge(f_loaded, 64 * (G - PAIRS + 1))
                    else:
                        pe.wait_ge(scores_used, START + UNITS * G + u - 1)
                    n = P * (i + 1)
                    qs = slice(P * i, P * i + P)
                    for c0 in range(0, n, HALF):
                        ks = slice(c0, min(c0 + HALF, n))
                        dst = scores[u % 2][:, ks]
                        pe.matmul(dst, q_hi[h][:, qs], k_st[h][:, ks], start=True, stop=False)
                        if fox:
                            pe.matmul(dst, q_f[h][:, qs], k_f[h][:, ks], start=False, stop=False)
                        if c0 + HALF >= n:
                            pe.matmul(scores[u % 2][:, n - P:n], ident_b[:, :], mask_b[int(fox)][:, :],
                                      start=False, stop=False)
                        mm = pe.matmul(dst, q_lo[h][:, qs], k_st[h][:, ks], start=False, stop=True)
                    mm.then_inc(scores_ready, 1)

                def turn_probs(u):
                    pe.wait_ge(probs_ready, UNITS * G + u + 1)
                    i = u % QB
                    for n, idx in enumerate(chunks_of(u)):
                        turn(idx, range(4 * n, min(4 * n + 4, i + 1)), prob[:, u % 2, :])

                def values(u):
                    h, i = divmod(u, QB)
                    pe.wait_ge(tp_free, START + TP_ITER * G + chunks_of(u)[-1] + 1)
                    pe.wait_ge(av_free, START + QB * G + u // 2)
                    if u == 1 and not fox:
                        pe.wait_ge(mod_made, G + 3)
                    for kb in range(i + 1):
                        q0 = P if kb == i else 0
                        for s in range(2):
                            mm = pe.matmul(ps[:, 6, q0:2 * P], v_st[:, kb, h, :, :].rearrange("p a d -> p (a d)"),
                                           wT[s][:, kb, q0:2 * P], start=(kb == 0 and s == 0), stop=(kb == i and s == 1))
                    mm.then_inc(av_done, 1)

                def gate_step(s):
                    if not 0 <= s < UNITS:
                        return
                    tile, hf, quarter = s // 8, s // 4 % 2, s % 4
                    b = 1 - tile
                    use = 2 * G + 1 if tile == 0 else 3 * G + 3
                    if s == 0:
                        pe.wait_ge(v_copied, 2 * G + 2)
                    elif quarter == 0:
                        pe.wait_ge(gate_copied, START + 4 * G + s // 4)
                    if quarter % 2 == 0:
                        pe.wait_ge(w_split[b], START + 2 * use + quarter // 2 + 1)
                    for k in (2 * quarter, 2 * quarter + 1):
                        mm = three(ps[:, 7, :], b, k, h1, halves[hf], k == 0, k == KT - 1)
                    if k == KT - 1:
                        mm.then_inc(gate_done, 1)

                for s in range(STEPS):
                    if s < UNITS:
                        score(s)
                    if s == 1:
                        turn_values()
                    if s >= 3 and s % 2 == 0:
                        values(s - 3)
                    if 2 <= s < UNITS + 2:
                        turn_probs(s - 2)
                    gate_step(s - GATE_LAG)

            with pe.Fori(0, PAIRS) as G:
                attend(G, False)
            with pe.Fori(PAIRS, 2 * PAIRS) as G:
                attend(G, True)

            pe.wait_ge(scores_used, START + 2 * PAIRS * UNITS)
            pe.wait_ge(tp_free, START + 2 * PAIRS * TP_ITER)
            pe.wait_ge(av_free, START + 2 * PAIRS * QB)
            pe.wait_ge(gate_copied, START + 8 * PAIRS)
            with pe.Fori(0, KT // 2) as n:
                for b in range(2):
                    pe.wait_ge(dense_free, FREE_MERGE - 2 + 2 * (2 * n + b))
                    for k in range(KT):
                        if k % 4 == 0:
                            pe.wait_ge(w_split[b], START + 2 * (USE_MERGE[b] + n) + k // 4 + 1)
                        pe.wait_ge(o_ready, k + 1)
                        for hf in range(2):
                            mm = three(ps[:, 4 * b + 2 * (k // 4) + hf, :], b, k, o_split, halves[hf],
                                       k % 4 == 0, k % 4 == 3)
                            if k % 4 == 3:
                                mm.then_inc(dense_done, 1)
            with pe.Fori(0, KT // 2) as n:
                for b in range(2):
                    pe.wait_ge(dense_free, FREE_WO - 2 + 2 * (2 * n + b))
                    dense(b, USE_WO[b] + n, merged, 2 * b, ready=lambda k: (dense_free, FREE_MERGE + 2 * k + 2))
            norm_stats(1, ss_b)
            with pe.Fori(0, FF_CHUNKS) as ch:
                with pe.Fori(0, KT // 2) as n:
                    for b in range(2):
                        pe.wait_ge(dense_free, FREE_FF + 2 * KT * ch)
                        pe.wait_ge(act_free, KT - 2 + 2 * KT * ch + 2 * (2 * n + b))
                        dense(b, USE_FF[b] + KT * ch + n, h2, 2 * b, ready=lambda k: (h_ready, 2 * KT + 2 * k + 2))
                with pe.Fori(0, KT // 2) as n:
                    for b in range(2):
                        pe.wait_ge(dense_free, FREE_FF - 2 + 2 * KT * ch + 2 * (2 * n + b))
                        pe.wait_ge(act_free, KT + 2 * KT * ch + 14 + 2 * b)
                        dense(b, USE_FF[b] + KT * ch + KT // 2 + n, hid, 2 * b,
                              ready=lambda k: (hid_ready, START + 2 * KT * ch + 2 * k + 2))
            norm_stats(2, ss_b)
            pe.wait_ge(y_ready, 2 * KT)
            for t in range(QB):
                if t >= 2:
                    pe.wait_ge(y_copied_act, t - 1)
                    pe.wait_ge(y_copied_dve, t - 1)
                for k in range(KT):
                    mm = pe.transpose(ps[:, 2 * (t % 2) + k // 4, P * (k % 4):P * (k % 4) + P],
                                      res[:, k, P * t:P * t + P], ident[:, :])
                    if k % 4 == 3:
                        mm.then_inc(y_turned, 1)

        @block.scalar
        def _(act):
            act.sem_inc(scores_used, START)
            act.sem_inc(gate_copied, START)
            for b in range(2):
                act.sem_inc(gate_saved[b], 16 * START)
            A = nc.scalar.activation
            halves = [slice(0, HALF), slice(HALF, T)]
            carrier = act.alloc_register("wait_carrier")
            carried = [0]

            def carry():
                carried[0] ^= 1
                act.reg_mov(carrier, carried[0])

            def square(which, n, src, sq):
                if n >= 2:
                    act.wait_ge(sq_summed, 2 * KT * which + n - 1)
                A(sq[:, n % 2, :], src[:, n // 2, halves[n % 2]], ACT.Square).then_inc(squared, 1)

            def root(which, rstd):
                act.wait_ge(stats_done, which + 1)
                A(rstd[:, :], ps[:, 4:6, :].rearrange("p a b -> p (a b)"), ACT.Sqrt, bias=eps_col[:, 0:1],
                  scale=1.0 / D).then_inc(root_done, 1)

            def norm_hi(which, n, tmp, h):
                act.wait_ge(normed, 2 * KT * which + n + 1)
                k = n // 2
                A(h[0][:, k, halves[n % 2]], tmp[:, n % 2, :], ACT.Identity,
                  bias=mod[:, 3 * KT * which + k:3 * KT * which + k + 1]).then_inc(h_hi, 1)

            act.wait_ge(consts_made, 6)
            for k in range(KT):
                act.wait_ge(x_turned, 2 * k + 1)
                A(xT[:, k, 0:HALF], ps[:, 2 * (k % 2), :], ACT.Copy).then_inc(x_kept_act, 1)
                act.wait_ge(x_kept_act, k + 1)
                square(0, 2 * k, xT, sq_a)
                act.wait_ge(x_kept_dve, k + 1)
                square(0, 2 * k + 1, xT, sq_a)
            root(0, rstd_a)
            act.wait_ge(mod_made, 1)
            for n in range(2 * KT):
                norm_hi(0, n, norm_a, h1)
            act.wait_ge(dense_done, DONE_F)
            A(f_abs[:, :], ps[0:HEADS, 2:4, :].rearrange("p a b -> p (a b)"), ACT.Abs,
              bias=bf_col[:, 0:1]).then_inc(f_step_act, 1)
            act.wait_ge(f_step_act, 1)
            A(f_abs[:, :], f_abs[:, :], ACT.Exp, scale=-1.0).then_inc(f_step_act, 1)
            act.wait_ge(f_step_act, 2)
            A(f_abs[:, :], f_abs[:, :], ACT.Ln, bias=ones[0:HEADS, 0:1]).then_inc(f_step_act, 1)
            act.wait_ge(f_step_dve, 8)
            act.dma_start(fparts_dram, f_parts[:, :, :]).then_inc(f_stored, 16)

            def attend(G, fox):
                done = DONE_F + DONE_ITER * G
                for hf in range(2):
                    act.wait_ge(dense_done, done + hf + 1)
                    A(k_st[0][0:DH, halves[hf]], ps[0:DH, hf, :], ACT.Copy)
                    A(k_st[1][DH:P, halves[hf]], ps[DH:P, hf, :], ACT.Copy).then_inc(k_hi_done, 1)
                for hf in range(2):
                    act.wait_ge(dense_done, done + 2 + hf + 1)
                    for h in range(2):
                        rows = slice(DH * h, DH * h + DH)
                        for to in range(2):
                            last = A(q_hi[h][DH * to:DH * to + DH, halves[hf]], ps[rows, 2 + hf, :], ACT.Copy, scale=SCALE)
                    last.then_inc(q_hi_done, 1)
                for hf in range(2):
                    act.wait_ge(dense_done, done + 4 + hf + 1)
                    act.wait_ge(gate_saved[hf], 16 * START + 32 * G)
                    A(vT[:, halves[hf]], ps[:, 6 + hf, :], ACT.Copy).then_inc(v_copied, 1)

                def values_hi():
                    for idx in range(V_CHUNKS):
                        act.wait_ge(tp_done, TP_ITER * G + idx + 1)
                        A(v_st[:, 4 * idx:4 * idx + 4, :, 0, :],
                          ps[:, 4 + idx, :].rearrange("p (b h d) -> p b h d", h=2, d=DH), ACT.Copy).then_inc(tp_hi, 1)

                def gate_out(q):
                    act.wait_ge(gate_done, START + 4 * G + q + 1)
                    act.wait_ge(gate_saved[q % 2], 16 * START + 16 * (2 * G + q // 2))
                    A(gate_st[:, q % 2, :], ps[:, 7, :], ACT.Copy).then_inc(gate_copied, 1)

                def gate_store(q):
                    act.wait_ge(gate_copied, START + 4 * G + q + 1)
                    act.dma_start(gates_dram[bass.ds(2 * G + q // 2, 1), :, halves[q % 2]].rearrange("a p t -> (a p) t"),
                                  gate_st[:, q % 2, :]).then_inc(gate_saved[q % 2], 16)

                def fold_values(u):
                    h = u // QB
                    own, other = slice(DH * h, DH * h + DH), slice(DH * (1 - h), DH * (1 - h) + DH)
                    act.wait_ge(av_done, START + QB * G + u // 2 + 1)
                    act.wait_ge(av_free, START + QB * G + u // 2)
                    A(fold[own, :], ps[other, 6, 0:2 * P], ACT.Copy).then_inc(av_folded, 1)

                def weights_hi(u):
                    i = u % QB
                    if i % 2 == 0:
                        act.wait_ge(av_done, START + QB * G + u // 2)
                    q0 = P * (i % 2)
                    for n, idx in enumerate(chunks_of(u)):
                        nb = min(4, i + 1 - 4 * n)
                        act.wait_ge(tp_done, TP_ITER * G + idx + 1)
                        A(wT[0][:, 4 * n:4 * n + nb, q0:q0 + P],
                          ps[:, 4 + idx % 2, 0:P * nb].rearrange("p (b q) -> p b q", q=P), ACT.Copy).then_inc(tp_hi, 1)

                def scores_out(u):
                    n = P * (u % QB + 1)
                    act.wait_ge(scores_ready, UNITS * G + u + 1)
                    if u >= 2:
                        act.wait_ge(tp_done, TP_ITER * G + chunks_of(u - 2)[-1] + 1)
                    z = scores[u % 2][:, 0:n]
                    if fox:
                        act.wait_ge(max_ready, UNITS * (G - PAIRS) + u + 1)
                        A(prob[:, u % 2, 0:n], z, ACT.Exp, bias=neg_max[:, u % 2:u % 2 + 1],
                          accum_out=row_sum[:, u % 2:u % 2 + 1]).then_inc(scores_used, 1)
                    else:
                        A(prob[:, u % 2, 0:n], z, ACT.Sigmoid)
                        A(surv[:, u % 2, 0:n], z, ACT.Sigmoid, scale=-1.0).then_inc(scores_used, 1)

                for s in range(STEPS):
                    q, at_q = divmod(s - GATE_LAG, 4)
                    if q >= 1 and at_q == 1:
                        gate_store(q - 1)
                    if q >= 1 and at_q == 0:
                        gate_out(q - 1)
                    if s == 1:
                        values_hi()
                    if s >= 3 and s % 2 == 0:
                        fold_values(s - 3)
                    if 2 <= s < UNITS + 2:
                        weights_hi(s - 2)
                    if s < UNITS:
                        scores_out(s)

            with act.Fori(0, PAIRS) as G:
                attend(G, False)
            with act.Fori(PAIRS, 2 * PAIRS) as G:
                attend(G, True)

            act.wait_ge(gate_done, START + 8 * PAIRS)
            act.wait_ge(av_free, START + 2 * PAIRS * QB)
            for k in range(KT):
                A(o_split[0][:, k, :], mixed[:, k, :], ACT.Copy).then_inc(o_hi_done, 1)
            for b in range(2):
                act.wait_ge(gate_saved[b], 16 * START + 16 * 4 * 2 * PAIRS // 2)

            def gates_back(tile, hf):
                for m in range(2):
                    act.dma_start(gates[:, hf, m, :],
                                  gates_dram[bass.ds(KT * m + tile, 1), :, halves[hf]].rearrange("a p t -> (a p) t")
                                  ).then_inc(gate_back[hf], 16)

            with act.Fori(0, KT) as n:
                for hf in range(2):
                    act.wait_ge(dense_free, FREE_MERGE - 1 + 2 * n + hf)
                    gates_back(n, hf)
                act.wait_ge(gate_back[0], 32 * n + 32)
                act.wait_ge(gate_back[1], 32 * n + 32)
                for m in range(2):
                    carry()
                    for hf in range(2):
                        A(gates[:, hf, m, :], gates[:, hf, m, :], ACT.Sigmoid,
                          bias=cols[:, bass.ds(COL_BGATE + KT * m + n, 1)]).then_inc(gate_on, 1)
                for hf in range(2):
                    act.wait_ge(merge_sum, 2 * n + hf + 1)
                    carry()
                    A(merged[0][:, bass.ds(n, 1), halves[hf]].rearrange("p a t -> p (a t)"), gates[:, hf, 0, :],
                      ACT.Copy).then_inc(merge_hi, 1)
            act.wait_ge(x_saved, 16)
            for k in range(KT):
                for hf in range(2):
                    act.wait_ge(dense_free, FREE_WO - 1 + 2 * k + hf if k else FREE_WO)
                    act.dma_start(x_again[:, hf, :], xT_dram[k, :, halves[hf]]).then_inc(x_back[hf], 16)
                if k:
                    for hf in range(2):
                        square(1, 2 * (k - 1) + hf, res, sq_b)
            for hf in range(2):
                act.wait_ge(dense_free, FREE_WO + 2 * (KT - 1) + hf + 1)
                square(1, 2 * (KT - 1) + hf, res, sq_b)
            root(1, rstd_b)
            for n in range(2 * KT):
                norm_hi(1, n, norm_b, h2)
                if n % 2:
                    k = n // 2
                    A(res[:, k, :], res[:, k, :], ACT.Identity, bias=gt_b[:, k:k + 1]).then_inc(act_free, 1)
            with act.Fori(0, FF_CHUNKS) as ch:
                with act.Fori(0, KT) as n:
                    for hf in range(2):
                        act.wait_ge(dense_done, DONE_FF + 4 * KT * ch + 2 * n + hf + 1)
                        act.wait_ge(hid_ready, START + 2 * KT * ch + 2 * n + hf)
                        carry()
                        A(relu[:, hf, :], ps[:, bass.ds(2 * (n % 2) + hf, 1), :].rearrange("p a t -> p (a t)"), ACT.Relu,
                          bias=cols[:, bass.ds(COL_BFF1 + KT * ch + n, 1)]).then_inc(act_free, 1)
                        act.wait_ge(act_free, KT + 2 * KT * ch + 2 * n + hf + 1)
                        carry()
                        A(hid[0][:, bass.ds(n, 1), halves[hf]].rearrange("p a t -> p (a t)"), relu[:, hf, :],
                          ACT.Square).then_inc(hid_hi, 1)
            for n in range(2 * KT):
                act.wait_ge(dense_free, FREE_FF + 2 * KT * (FF_CHUNKS - 1) + n + 1)
                square(2, n, res, sq_b)
            root(2, rstd_b)
            for t in range(QB):
                act.wait_ge(y_turned, 2 * t + 1)
                if t >= 2:
                    act.wait_ge(out_saved[t % 2], 16 * (t // 2))
                A(out_st[:, t % 2, 0:HALF], ps[:, 2 * (t % 2), :], ACT.Copy).then_inc(y_copied_act, 1)

        @block.vector
        def _(dve):
            dve.sem_inc(av_free, START)
            dve.sem_inc(tp_free, START)
            dve.sem_inc(hid_ready, START)
            V = nc.vector
            halves = [slice(0, HALF), slice(HALF, T)]

            def ada_step(m, k, first=False):
                use = KT // 2 * m + k // 2
                dve.wait_ge(ada_loaded[k % 2], 16 * use + 16)
                ck = cols[:, COL_C + k:COL_C + k + 1]
                if k == 0:
                    if not first:
                        dve.wait_ge(ada_summed, m)
                    V.tensor_scalar(ada_sum[:, :], ada[:, 0, :], ck, None, ALU.mult).then_inc(ada_used, 1)
                else:
                    dve.wait_ge(ada_used, KT * m + k)
                    V.scalar_tensor_tensor(out=ada_sum[:, :], in0=ada[:, k % 2, :], scalar=ck, in1=ada_sum[:, :],
                                           op0=ALU.mult, op1=ALU.add).then_inc(ada_used, 1)

            def mod_cols(m):
                dve.wait_ge(ada_summed, m + 1)
                V.tensor_tensor(mod[:, bass.ds(KT * m, KT)], ps[:, 6, 0:KT], cols[:, bass.ds(COL_BADA + KT * m, KT)],
                                ALU.add).then_inc(mod_made, 1)

            def add_square(which, n, ss, sq):
                dve.wait_ge(squared, 2 * KT * which + n + 1)
                half = ss[:, halves[n % 2]]
                if n < 2:
                    ins = V.tensor_copy(half, sq[:, n % 2, :])
                else:
                    dve.wait_ge(sq_summed, 2 * KT * which + n - 1)
                    ins = V.tensor_tensor(half, half, sq[:, n % 2, :], ALU.add)
                ins.then_inc(sq_summed, 1)

            def invert(which, rstd):
                dve.wait_ge(root_done, which + 1)
                V.reciprocal(rstd[:, :], rstd[:, :]).then_inc(rstd_made, 1)
                dve.wait_ge(rstd_made, which + 1)

            def norm_tiles(which, src, rstd, tmp, h):
                def scaled(n):
                    if n >= 2:
                        dve.wait_ge(h_ready, 2 * KT * which + n - 1)
                    V.scalar_tensor_tensor(out=tmp[:, n % 2, :], in0=src[:, n // 2, halves[n % 2]],
                                           scalar=g_sc[which][:, n // 2:n // 2 + 1], in1=rstd[:, halves[n % 2]],
                                           op0=ALU.mult, op1=ALU.mult).then_inc(normed, 1)

                def rest(n):
                    dve.wait_ge(h_hi, 2 * KT * which + n + 1)
                    k = n // 2
                    V.scalar_tensor_tensor(out=h[1][:, k, halves[n % 2]], in0=tmp[:, n % 2, :],
                                           scalar=mod[:, 3 * KT * which + k:3 * KT * which + k + 1],
                                           in1=h[0][:, k, halves[n % 2]].bitcast(F32),
                                           op0=ALU.add, op1=ALU.subtract).then_inc(h_ready, 1)

                for n in range(2 * KT):
                    scaled(n)
                    if n:
                        rest(n - 1)
                rest(2 * KT - 1)

            dve.wait_ge(pack_turned, 1)
            V.tensor_copy(cols[:, :], ps[:, 6, 0:PACK1 + PACK2]).then_inc(cols_made, 1)
            dve.wait_ge(cols_made, 1)
            for k in range(KT):
                dve.wait_ge(x_turned, 2 * k + 2)
                V.tensor_copy(xT[:, k, HALF:T], ps[:, 2 * (k % 2) + 1, :]).then_inc(x_kept_dve, 1)
                if k:
                    add_square(0, 2 * k - 2, ss_a, sq_a)
                    add_square(0, 2 * k - 1, ss_a, sq_a)
            add_square(0, 2 * KT - 2, ss_a, sq_a)
            add_square(0, 2 * KT - 1, ss_a, sq_a)
            for k in range(KT):
                ada_step(0, k, first=True)
            mod_cols(0)
            for k in range(KT):
                ada_step(1, k)
            mod_cols(1)
            dve.wait_ge(mod_made, 2)
            V.scalar_tensor_tensor(out=g_sc[0][:, :], in0=mod[:, KT:2 * KT], scalar=1.0, in1=cols[:, COL_GMIX:COL_GMIX + KT],
                                   op0=ALU.add, op1=ALU.mult).then_inc(mod_derived, 1)
            dve.wait_ge(mod_derived, 1)
            invert(0, rstd_a)
            norm_tiles(0, xT, rstd_a, norm_a, h1)

            fl = ps[0:HEADS, 2:4, :].rearrange("p a b -> p (a b)")
            dve.wait_ge(f_step_act, 1)
            V.tensor_scalar(f_log[:, 0:HALF], fl[:, 0:HALF], bf_col[:, 0:1], 0.0, ALU.add, ALU.min).then_inc(dense_free, 1)
            V.tensor_scalar(f_log[:, HALF:T], fl[:, HALF:T], bf_col[:, 0:1], 0.0, ALU.add, ALU.min).then_inc(dense_free, 1)
            dve.wait_ge(dense_free, FREE_F)
            dve.wait_ge(f_step_act, 3)
            V.tensor_tensor(f_log[:, :], f_log[:, :], f_abs[:, :], ALU.subtract).then_inc(f_step_dve, 1)
            dve.wait_ge(f_step_dve, 1)
            V.tensor_tensor_scan(f_cum[:, :], f_log[:, :], ones[0:HEADS, 0:1].to_broadcast([HEADS, T]), 0.0,
                                 ALU.add, ALU.mult).then_inc(f_step_dve, 1)
            dve.wait_ge(f_step_dve, 2)
            part = f_cum
            for n in range(3):
                V.tensor_copy(f_parts[:, n, :], part[:, :]).then_inc(f_step_dve, 1)
                dve.wait_ge(f_step_dve, 3 + 2 * n)
                V.tensor_tensor(f_rest[:, :], part[:, :], f_parts[:, n, :], ALU.subtract).then_inc(f_step_dve, 1)
                dve.wait_ge(f_step_dve, 4 + 2 * n)
                part = f_rest

            def attend(G, fox):
                if not fox:
                    for k in range(4):
                        ada_step(G + 2, k)
                for hf in range(2):
                    dve.wait_ge(k_hi_done, 2 * G + hf + 1)
                    for h in range(2):
                        own, other = slice(DH * h, DH * h + DH), slice(DH * (1 - h), DH * (1 - h) + DH)
                        last = V.tensor_tensor(k_st[h][other, halves[hf]], ps[own, hf, :],
                                               k_st[h][own, halves[hf]].bitcast(F32), ALU.subtract)
                    last.then_inc(dense_free, 1)
                for hf in range(2):
                    dve.wait_ge(q_hi_done, 2 * G + hf + 1)
                    for h in range(2):
                        own = slice(DH * h, DH * h + DH)
                        for to in range(2):
                            last = V.scalar_tensor_tensor(
                                out=q_lo[h][DH * to:DH * to + DH, halves[hf]], in0=ps[own, 2 + hf, :], scalar=SCALE,
                                in1=q_hi[h][own, halves[hf]].bitcast(F32), op0=ALU.mult, op1=ALU.subtract)
                    last.then_inc(dense_free, 1)
                if not fox:
                    for k in range(4, KT):
                        ada_step(G + 2, k)

                def values_lo():
                    for idx in range(V_CHUNKS):
                        dve.wait_ge(tp_hi, TP_ITER * G + idx + 1)
                        V.tensor_tensor(v_st[:, 4 * idx:4 * idx + 4, :, 1, :],
                                        ps[:, 4 + idx, :].rearrange("p (b h d) -> p b h d", h=2, d=DH),
                                        v_st[:, 4 * idx:4 * idx + 4, :, 0, :].bitcast(F32), ALU.subtract).then_inc(tp_free, 1)
                    if not fox:
                        mod_cols(G + 2)
                        dve.wait_ge(f_stored, 16)

                def add_values(u):
                    h, i = divmod(u, QB)
                    own = slice(DH * h, DH * h + DH)
                    dve.wait_ge(av_folded, QB * G + u // 2 + 1)
                    q0 = P * (i - 1)
                    V.tensor_tensor(mixed[own, bass.ds(G, 1), q0:q0 + 2 * P].rearrange("p a t -> p (a t)"),
                                    ps[own, 6, 0:2 * P], fold[own, :], ALU.add).then_inc(av_free, 1)

                def weights_lo(u):
                    i = u % QB
                    q0 = P * (i % 2)
                    for n, idx in enumerate(chunks_of(u)):
                        nb = min(4, i + 1 - 4 * n)
                        dve.wait_ge(tp_hi, TP_ITER * G + idx + 1)
                        V.tensor_tensor(wT[1][:, 4 * n:4 * n + nb, q0:q0 + P],
                                        ps[:, 4 + idx % 2, 0:P * nb].rearrange("p (b q) -> p b q", q=P),
                                        wT[0][:, 4 * n:4 * n + nb, q0:q0 + P].bitcast(F32),
                                        ALU.subtract).then_inc(tp_free, 1)

                def row_max(u):
                    n = P * (u % QB + 1)
                    dve.wait_ge(scores_ready, UNITS * G + u + 1)
                    V.tensor_reduce(neg_max[:, u % 2:u % 2 + 1], scores[u % 2][:, 0:n], AX.X, ALU.max,
                                    negate=True).then_inc(max_ready, 1)

                def finish_weights(u):
                    n = P * (u % QB + 1)
                    dve.wait_ge(scores_used, START + UNITS * G + u + 1)
                    pr = prob[:, u % 2, 0:n]
                    if fox:
                        V.reciprocal(inv_sum[:, u % 2:u % 2 + 1], row_sum[:, u % 2:u % 2 + 1]).then_inc(inv_ready, 1)
                        dve.wait_ge(inv_ready, UNITS * (G - PAIRS) + u + 1)
                        V.tensor_scalar(pr, pr, inv_sum[:, u % 2:u % 2 + 1], None, ALU.mult).then_inc(probs_ready, 1)
                    else:
                        sv = surv[:, u % 2, 0:n]
                        V.tensor_tensor_scan(sv[:, ::-1], sv[:, ::-1], ones[:, 0:1].to_broadcast([P, n]), 1.0, ALU.mult,
                                             ALU.mult).then_inc(scanned, 1)
                        dve.wait_ge(scanned, UNITS * G + u + 1)
                        V.tensor_tensor(pr[:, 0:n - 1], pr[:, 0:n - 1], sv[:, 1:n], ALU.mult).then_inc(probs_ready, 1)

                for s in range(STEPS):
                    if fox and s < UNITS:
                        row_max(s)
                    if s == 1:
                        values_lo()
                    if s >= 3 and s % 2 == 0:
                        add_values(s - 3)
                    if 2 <= s < UNITS + 2:
                        weights_lo(s - 2)
                    if s < UNITS:
                        finish_weights(s)

            with dve.Fori(0, PAIRS) as G:
                attend(G, False)
            dve.wait_ge(mod_made, N_MOD)
            for h in range(2):
                V.memset(q_f[h][:, :], -1.0).then_inc(f_ones, 1)
                V.memset(k_f[h][:, :], 1.0).then_inc(f_ones, 1)
            V.scalar_tensor_tensor(out=g_sc[1][:, :], in0=mod[:, 4 * KT:5 * KT], scalar=1.0, in1=cols[:, COL_GMLP:COL_GMLP + KT],
                                   op0=ALU.add, op1=ALU.mult).then_inc(mod_derived, 1)
            V.tensor_tensor(gt_b[:, :], mod[:, 5 * KT:6 * KT], cols[:, COL_BFF2:COL_BFF2 + KT], ALU.mult).then_inc(mod_derived, 1)
            dve.wait_ge(mod_derived, 3)
            with dve.Fori(PAIRS, 2 * PAIRS) as G:
                attend(G, True)

            for k in range(KT):
                dve.wait_ge(o_hi_done, k + 1)
                V.tensor_tensor(o_split[1][:, k, :], mixed[:, k, :], o_split[0][:, k, :].bitcast(F32),
                                ALU.subtract).then_inc(o_ready, 1)
            with dve.Fori(0, KT // 2) as n:
                for b in range(2):
                    for hf in range(2):
                        step = 4 * n + 2 * b + hf
                        for m in range(2):
                            dve.wait_ge(gate_on, 8 * n + 4 * b + 2 * m + hf + 1)
                            dve.wait_ge(dense_done, DONE_MERGE + 8 * n + 4 * b + 2 * m + hf + 1)
                            V.tensor_tensor(gates[:, hf, m, :], ps[:, 4 * b + 2 * m + hf, :], gates[:, hf, m, :],
                                            ALU.mult).then_inc(merge_mul, 1)
                        dve.wait_ge(merge_mul, 2 * step + 2)
                        V.tensor_tensor(gates[:, hf, 0, :], gates[:, hf, 0, :], gates[:, hf, 1, :],
                                        ALU.add).then_inc(merge_sum, 1)
                        dve.wait_ge(merge_hi, step + 1)
                        V.tensor_tensor(merged[1][:, bass.ds(2 * n + b, 1), halves[hf]].rearrange("p a t -> p (a t)"),
                                        gates[:, hf, 0, :],
                                        merged[0][:, bass.ds(2 * n + b, 1), halves[hf]].rearrange("p a t -> p (a t)").bitcast(F32),
                                        ALU.subtract).then_inc(dense_free, 1)
            for k in range(KT):
                for hf in range(2):
                    dve.wait_ge(dense_done, DONE_WO + 2 * k + hf + 1)
                    dve.wait_ge(x_back[hf], 16 * k + 16)
                    V.scalar_tensor_tensor(out=res[:, k, halves[hf]], in0=ps[:, 2 * (k % 2) + hf, :],
                                           scalar=mod[:, 2 * KT + k:2 * KT + k + 1], in1=x_again[:, hf, :],
                                           op0=ALU.mult, op1=ALU.add).then_inc(dense_free, 1)
                if k:
                    add_square(1, 2 * k - 2, ss_b, sq_b)
                    add_square(1, 2 * k - 1, ss_b, sq_b)
            add_square(1, 2 * KT - 2, ss_b, sq_b)
            add_square(1, 2 * KT - 1, ss_b, sq_b)
            invert(1, rstd_b)
            norm_tiles(1, res, rstd_b, norm_b, h2)
            dve.wait_ge(act_free, KT)
            with dve.Fori(0, FF_CHUNKS) as ch:
                with dve.Fori(0, KT) as n:
                    for hf in range(2):
                        step = 2 * KT * ch + 2 * n + hf
                        dve.wait_ge(act_free, KT + step + 1)
                        V.tensor_tensor(relu_sq[:, hf, :], relu[:, hf, :], relu[:, hf, :], ALU.mult).then_inc(relu_squared, 1)
                        dve.wait_ge(relu_squared, step + 1)
                        dve.wait_ge(hid_hi, step + 1)
                        V.tensor_tensor(hid[1][:, bass.ds(n, 1), halves[hf]].rearrange("p a t -> p (a t)"), relu_sq[:, hf, :],
                                        hid[0][:, bass.ds(n, 1), halves[hf]].rearrange("p a t -> p (a t)").bitcast(F32),
                                        ALU.subtract).then_inc(hid_ready, 1)
                with dve.Fori(0, KT // 2) as n:
                    for b in range(2):
                        for hf in range(2):
                            step = 2 * KT * ch + 4 * n + 2 * b + hf
                            dve.wait_ge(dense_done, DONE_FF + 4 * KT * ch + 2 * KT + 4 * n + 2 * b + hf + 1)
                            dve.wait_ge(dense_free, FREE_FF - 2 * KT + step + 1)
                            tile = res[:, bass.ds(2 * n + b, 1), halves[hf]].rearrange("p a t -> p (a t)")
                            V.scalar_tensor_tensor(out=tile, in0=ps[:, 2 * b + hf, :],
                                                   scalar=mod[:, bass.ds(5 * KT + 2 * n + b, 1)], in1=tile,
                                                   op0=ALU.mult, op1=ALU.add).then_inc(dense_free, 1)
            for n in range(2 * KT):
                add_square(2, n, ss_b, sq_b)
            invert(2, rstd_b)
            for n in range(2 * KT):
                tile = res[:, n // 2, halves[n % 2]]
                V.scalar_tensor_tensor(out=tile, in0=tile, scalar=cols[:, COL_GFIN + n // 2:COL_GFIN + n // 2 + 1],
                                       in1=rstd_b[:, halves[n % 2]], op0=ALU.mult, op1=ALU.mult).then_inc(y_ready, 1)
            for t in range(QB):
                dve.wait_ge(y_turned, 2 * t + 2)
                if t >= 2:
                    dve.wait_ge(out_saved[t % 2], 16 * (t // 2))
                V.tensor_copy(out_st[:, t % 2, HALF:T], ps[:, 2 * (t % 2) + 1, :]).then_inc(y_copied_dve, 1)


_INS = ["x", "c", "w_ada", "b_ada", "g_mix", "w_in", "b_f", "w_gate", "b_gate", "w_out_sb", "w_out_fox",
        "w_o", "g_mlp", "w_ff1", "b_ff1", "w_ff2", "b_ff2", "g_final"]


def kernel(**inputs):
    import numpy as np
    import concourse.bacc as bacc
    from concourse.bass_utils import run_bass_kernel_spmd

    nc = bacc.Bacc("TRN2", target_bir_lowering=False, num_devices=1)
    arrays, args = {}, []
    for name in _INS:
        a = np.ascontiguousarray(inputs[name])
        arrays[f"in_{name}"] = a
        args.append(nc.dram_tensor(f"in_{name}", a.shape, mybir.dt.from_np(a.dtype), kind="ExternalInput").ap())
    shape = inputs["x"].shape
    args.append(nc.dram_tensor("out_0", shape, F32, kind="ExternalOutput").ap())
    build_block(nc, *args)
    r = run_bass_kernel_spmd(nc, [arrays], core_ids=[0])
    return r.results[0]["out_0"]
```

```python
from contextlib import ExitStack

import concourse.bass as bass
from concourse import mybir

P = 128
D = 1024
T = 1024
KT = D // P
HALF = 512
HEADS = 8
DH = 64
D_MIX = HEADS * DH
D_FF = 4 * D
N_MOD = 6
QB = T // P
PAIRS = HEADS // 2
UNITS = 2 * QB
EPS = 1e-6
SCALE = DH ** -0.5
NEG = -1.0e30
FF_CHUNKS = 4

F32 = mybir.dt.float32
F32R = mybir.dt.float32r
BF16 = mybir.dt.bfloat16
ALU = mybir.AluOpType
ACT = mybir.ActivationFunctionType
AX = mybir.AxisListType

COL_GMIX, COL_GMLP, COL_BGATE, COL_BFF1, COL_C, COL_GFIN, COL_BFF2, COL_BADA = 0, 8, 16, 32, 64, 72, 80, 88
PACK1 = COL_BADA
PACK2 = N_MOD * KT

DONE_F, DONE_ITER = 2, 6
DONE_MERGE = DONE_F + 2 * PAIRS * DONE_ITER
DONE_WO = DONE_MERGE + 4 * KT
DONE_FF = DONE_WO + 2 * KT
FREE_F, FREE_ITER = 2, 4
FREE_MERGE = FREE_F + 2 * PAIRS * FREE_ITER
FREE_WO = FREE_MERGE + 2 * KT
FREE_FF = FREE_WO + 2 * KT
FREE_LAST = FREE_FF + 2 * KT * (FF_CHUNKS - 1)
START = 1
USE_MERGE = (3 * 2 * PAIRS, 2 * 2 * PAIRS)
USE_WO = (USE_MERGE[0] + KT // 2, USE_MERGE[1] + KT // 2)
USE_FF = (USE_WO[0] + KT // 2, USE_WO[1] + KT // 2)
V_CHUNKS = 2


def chunks_of(u):
    first = V_CHUNKS
    for w in range(u):
        first += 1 if w % QB < 4 else 2
    return list(range(first, first + (1 if u % QB < 4 else 2)))


TP_ITER = chunks_of(UNITS - 1)[-1] + 1
GATE_LAG = 1
STEPS = UNITS + 3


def build_block(nc, x, c, w_ada, b_ada, g_mix, w_in, b_f, w_gate, b_gate, w_out_sb, w_out_fox,
                w_o, g_mlp, w_ff1, b_ff1, w_ff2, b_ff2, g_final, out):
    x_rows = x.rearrange("b (t p) d -> (b t) p d", p=P)
    out_rows = out.rearrange("b (t p) d -> (b t) p d", p=P)
    tiles_of = lambda w: w.rearrange("l (k p) n -> p (l k) n", p=P)
    ada_t, in_t, gate_t, wo_t, ff1_t = map(tiles_of, (w_ada, w_in, w_gate, w_o, w_ff1))
    osb_t, ofx_t, ff2_t = map(tiles_of, (w_out_sb, w_out_fox, w_ff2))
    rows_of = lambda v: v.rearrange("l (r q) -> (l r) q", q=P)
    xT_dram = nc.dram_tensor("xT_dram", [KT, P, T], F32, kind="Internal").ap()
    gates_dram = nc.dram_tensor("gates_dram", [2 * KT, P, T], F32, kind="Internal").ap()
    fparts_dram = nc.dram_tensor("fparts_dram", [HEADS, 3, T], BF16, kind="Internal").ap()

    base = (nc.sbuf_base + 31) // 32 * 32
    KB = 1024
    R1, R2, R3, R4, R5, R6 = (base + n * KB for n in (0, 64, 128, 160, 184, 196))
    R7 = base + 204 * KB

    def at(name, offset, shape, dtype):
        return nc.alloc_sbuf_tensor_at(name, shape, dtype, offset=offset)

    h1 = [at(f"h1_{s}", R1 + n * 32 * KB, [P, KT, T], F32R) for n, s in enumerate(("hi", "lo"))]
    o_split = [at(f"o_{s}", R1 + n * 32 * KB, [P, KT, T], F32R) for n, s in enumerate(("hi", "lo"))]
    h2 = [at(f"h2_{s}", R1 + n * 32 * KB, [P, KT, T], F32R) for n, s in enumerate(("hi", "lo"))]
    ada_first = at("ada_first", R1, [P, 2 * KT, D], F32)
    y_nat = at("y_nat", R1, [P, QB, D], F32)
    gain_row = at("gain_row", R1 + 32 * KB, [P, D], F32)
    x_in = at("x_in", R2, [P, KT, T], F32)
    x_scaled = at("x_scaled", R2, [P, KT, T], F32)
    sq_a = at("sq_a", R2 + 32 * KB, [P, 2, D], F32)
    diag = at("diag", R2 + 40 * KB, [P, QB, P], F32)
    pack1 = at("pack1", R2 + 48 * KB, [PACK1, P], F32)
    pack2 = at("pack2", R2 + 49 * KB, [PACK2, P], F32)
    q_hi = [at(f"q_hi{h}", R2 + 4 * h * KB, [P, T], F32R) for h in range(2)]
    q_lo = [at(f"q_lo{h}", R2 + (8 + 4 * h) * KB, [P, T], F32R) for h in range(2)]
    k_st = [at(f"k_st{h}", R2 + (16 + 4 * h) * KB, [P, T], F32R) for h in range(2)]
    v_st = at("v_st", R2 + 24 * KB, [P, QB, 2, 2, DH], F32R)
    prob = at("prob", R2 + 32 * KB, [P, 2, T], F32)
    surv = at("surv", R2 + 40 * KB, [P, 2, T], F32)
    wT = [at(f"wT_{s}", R2 + (48 + 8 * n) * KB, [P, QB, 2 * P], F32R) for n, s in enumerate(("hi", "lo"))]
    f_abs = at("f_abs", R2 + 40 * KB, [HEADS, T], F32)
    f_log = at("f_log", R2 + 44 * KB, [HEADS, T], F32)
    f_cum = at("f_cum", R2 + 48 * KB, [HEADS, T], F32)
    f_rest = at("f_rest", R2 + 52 * KB, [HEADS, T], F32)
    f_parts = at("f_parts", R2 + 56 * KB, [HEADS, 3, T], BF16)
    merged = [at(f"merged_{s}", R2 + n * 32 * KB, [P, KT, T], F32R) for n, s in enumerate(("hi", "lo"))]
    hid = [at(f"hid_{s}", R2 + n * 32 * KB, [P, KT, T], F32R) for n, s in enumerate(("hi", "lo"))]
    xT = at("xT", R3, [P, KT, T], F32)
    mixed = at("mixed", R3, [P, KT, T], F32)
    res = at("res", R3, [P, KT, T], F32)
    w_raw = [at(f"w_raw{b}", R4 + 4 * b * KB, [P, KT, P], F32) for b in range(2)]
    w_hi = [at(f"w_hi{b}", R4 + (8 + 4 * b) * KB, [P, KT, P], F32R) for b in range(2)]
    w_lo = [at(f"w_lo{b}", R4 + (16 + 4 * b) * KB, [P, KT, P], F32R) for b in range(2)]
    ada = at("ada", R5, [P, 2, D], F32)
    ada_sum = at("ada_sum", R5 + 8 * KB, [P, D], F32)
    q_f = [at(f"q_f{h}", R5 + 4 * h * KB, [6, T], BF16) for h in range(2)]
    k_f = [at(f"k_f{h}", R5 + (4 * h + 2) * KB, [6, T], BF16) for h in range(2)]
    gates = at("gates", R5, [P, 2, 2, T], F32)
    ss_b = at("ss_b", R5, [P, T], F32)
    rstd_b = at("rstd_b", R5 + 4 * KB, [P, T], F32)
    sq_b = at("sq_b", R5 + 8 * KB, [P, 2, HALF], F32)
    gate_st = at("gate_st", R6, [P, 2, HALF], F32)
    vT = at("vT", R6, [P, T], F32)
    fold = at("fold", R6 + 4 * KB, [P, 2 * P], F32)
    x_again = at("x_again", R6 + 4 * KB, [P, 2, HALF], F32)
    norm_b = at("norm_b", R6, [P, 2, T], F32)
    relu = at("relu", R6, [P, 2, HALF], F32)
    relu_sq = at("relu_sq", R6 + 4 * KB, [P, 2, HALF], F32)
    y_st = at("y_st", R6, [P, 2, T], F32)
    spot = [R7]

    def small(name, shape, dtype):
        n = 1
        for s in shape[1:]:
            n *= s
        t = at(name, spot[0], shape, dtype)
        spot[0] += (n * (2 if dtype == BF16 else 4) + 31) // 32 * 32
        assert spot[0] <= nc.sbuf_usable_end
        return t

    ident = small("ident", [P, P], F32)
    ones = small("ones", [P, P], F32)
    ident_b = small("ident_b", [P, P], BF16)
    mask_b = [small(f"mask_b{m}", [P, P], BF16) for m in range(2)]
    cols = small("cols", [P, PACK1 + PACK2], F32)
    mod = small("mod", [P, N_MOD * KT], F32)
    g_sc = [small(f"g_sc{n}", [P, KT], F32) for n in range(2)]
    gt_b = small("gt_b", [P, KT], F32)
    w_f_raw = small("w_f_raw", [P, KT, HEADS], F32)
    w_f_hi = small("w_f_hi", [P, KT, HEADS], F32R)
    w_f_lo = small("w_f_lo", [P, KT, HEADS], F32R)
    eps_col = small("eps_col", [P, 1], F32)
    rms_a = small("rms_a", [P, QB], F32)
    rstd_a = small("rstd_a", [P, QB], F32)
    rms_c = small("rms_c", [P, QB], F32)
    rstd_c = small("rstd_c", [P, QB], F32)
    bf_col = small("bf_col", [HEADS, 1], F32)
    neg_max = small("neg_max", [P, 2], F32)
    row_sum = small("row_sum", [P, 2], F32)
    inv_sum = small("inv_sum", [P, 2], F32)

    with ExitStack() as ctx:
        ps = ctx.enter_context(nc.psum_tensor("ps", [P, 8, HALF], F32))
        scores = [ps[:, 2 * s:2 * s + 2, :].rearrange("p a b -> p (a b)") for s in range(2)]
        sem = lambda name: ctx.enter_context(nc.semaphore(name))

        consts_made = sem("consts_made")
        identity_made = sem("identity_made")
        small_loaded = sem("small_loaded")
        x_loaded = [sem(f"x_loaded{t}") for t in range(QB)]
        x_squared, diag_made, rstd_spread = sem("x_squared"), sem("diag_made"), sem("rstd_spread")
        ada_in = [sem(f"ada_in{j}") for j in range(KT)]
        pack_turned, cols_made = sem("pack_turned"), sem("cols_made")
        ada_loaded = [sem(f"ada_loaded{b}") for b in range(2)]
        ada_used, ada_summed, mod_made, mod_derived = (sem(n) for n in ("ada_used", "ada_summed", "mod_made", "mod_derived"))
        x_turned, x_kept_act, x_kept_dve, x_saved = (sem(n) for n in ("x_turned", "x_kept_act", "x_kept_dve", "x_saved"))
        squared, sq_summed, stats_done, root_done, rstd_made = (
            sem(n) for n in ("squared", "sq_summed", "stats_done", "root_done", "rstd_made"))
        normed, h_hi, h_ready = sem("normed"), sem("h_hi"), sem("h_ready")
        w_loaded = [sem(f"w_loaded{b}") for b in range(2)]
        hi_split = [sem(f"hi_split{b}") for b in range(2)]
        w_split = [sem(f"w_split{b}") for b in range(2)]
        f_w_loaded, f_w_split = sem("f_w_loaded"), sem("f_w_split")
        dense_done, dense_free = sem("dense_done"), sem("dense_free")
        f_step_dve, f_step_act, f_stored, f_loaded, f_ones = (
            sem(n) for n in ("f_step_dve", "f_step_act", "f_stored", "f_loaded", "f_ones"))
        v_copied, k_hi_done, q_hi_done = sem("v_copied"), sem("k_hi_done"), sem("q_hi_done")
        scores_ready, scores_used = sem("scores_ready"), sem("scores_used")
        scanned, max_ready, inv_ready, probs_ready = (sem(n) for n in ("scanned", "max_ready", "inv_ready", "probs_ready"))
        tp_done, tp_hi, tp_free = sem("tp_done"), sem("tp_hi"), sem("tp_free")
        av_done, av_folded, av_free = sem("av_done"), sem("av_folded"), sem("av_free")
        gate_done, gate_copied = sem("gate_done"), sem("gate_copied")
        gate_saved = [sem(f"gate_saved{b}") for b in range(2)]
        gate_back = [sem(f"gate_back{b}") for b in range(2)]
        o_hi_done, o_ready = sem("o_hi_done"), sem("o_ready")
        gate_on, merge_mul, merge_sum, merge_hi = (sem(n) for n in ("gate_on", "merge_mul", "merge_sum", "merge_hi"))
        x_back = [sem(f"x_back{b}") for b in range(2)]
        act_free, hid_hi, relu_squared, hid_ready = (sem(n) for n in ("act_free", "hid_hi", "relu_squared", "hid_ready"))
        gain_loaded, y_turned, y_kept, out_saved = (sem(n) for n in ("gain_loaded", "y_turned", "y_kept", "out_saved"))
        y_scaled = [sem(f"y_scaled{b}") for b in range(2)]

        block = ctx.enter_context(nc.Block())

        @block.sync
        def _(sp):
            for r, v in ((COL_GMIX, g_mix), (COL_GMLP, g_mlp), (COL_BGATE, b_gate), (COL_BFF1, b_ff1),
                         (COL_C, c), (COL_GFIN, g_final.rearrange("(l d) -> l d", l=1)), (COL_BFF2, b_ff2)):
                src = rows_of(v)
                sp.dma_start(pack1[r:r + src.shape[0], :], src).then_inc(small_loaded, 16)
            sp.dma_start(pack2[:, :], rows_of(b_ada)).then_inc(small_loaded, 16)
            sp.dma_start(bf_col[:, :], b_f.rearrange("l h -> h l")).then_inc(small_loaded, 16)
            for t in range(KT):
                sp.dma_start(x_in[:, t, :], x_rows[t]).then_inc(x_loaded[t], 16)
            for j in range(KT):
                m, k = 1 - 2 * j // KT, 2 * j % KT
                sp.dma_start(ada_first[:, 2 * j:2 * j + 2, :], ada_t[:, k:k + 2, D * m:D * m + D]).then_inc(ada_in[j], 16)
            sp.dma_start(w_f_raw[:, :, :], in_t[:, :, 6 * D_MIX:6 * D_MIX + HEADS]).then_inc(f_w_loaded, 16)

            def load_ada(m, k):
                sp.wait_ge(ada_used, KT * m + k - 1)
                sp.dma_start(ada[:, k % 2, :], ada_t[:, k, bass.ds(D * m, D)]).then_inc(ada_loaded[k % 2], 16)

            def load_w(b, use, parts):
                sp.wait_ge(w_split[b], START + 2 * use)
                for hf in (1, 0):
                    sp.dma_start(w_raw[b][:, 4 * hf:4 * hf + 4, :], parts[hf]).then_inc(w_loaded[b], 16)

            halves = lambda w, col: [w[:, 0:4, bass.ds(col, P)], w[:, 4:8, bass.ds(col, P)]]

            def pair_loads(G, k_col, q_col, v_col, fox):
                load_w(0, 3 * G, halves(in_t, k_col))
                if not fox:
                    load_ada(G + 2, 0)
                    load_ada(G + 2, 1)
                load_w(1, 2 * G, halves(in_t, q_col))
                if not fox:
                    load_ada(G + 2, 2)
                    load_ada(G + 2, 3)
                else:
                    sp.wait_ge(f_stored, 16)
                    sp.wait_ge(f_ones, 4)
                    sp.wait_ge(scores_ready, UNITS * G)
                    for h in range(2):
                        src = fparts_dram[bass.ds(2 * (G - PAIRS) + h, 1)].rearrange("a r t -> (a r) t")
                        sp.dma_start(q_f[h][0:3, :], src).then_inc(f_loaded, 16)
                        sp.dma_start(k_f[h][3:6, :], src).then_inc(f_loaded, 16)
                load_w(0, 3 * G + 1, halves(in_t, v_col))
                if not fox:
                    load_ada(G + 2, 4)
                    load_ada(G + 2, 5)
                load_w(1, 2 * G + 1, halves(gate_t, 2 * P * G))
                if not fox:
                    load_ada(G + 2, 6)
                    load_ada(G + 2, 7)
                load_w(0, 3 * G + 2, halves(gate_t, 2 * P * G + P))

            with sp.Fori(0, PAIRS) as G:
                pair_loads(G, D_MIX + P * G, P * G, 2 * D_MIX + P * G, False)
            with sp.Fori(PAIRS, 2 * PAIRS) as G:
                at_g = 3 * D_MIX - P * PAIRS + P * G
                pair_loads(G, at_g + D_MIX, at_g, at_g + 2 * D_MIX, True)
            for n in range(KT):
                load_w(n % 2, USE_MERGE[n % 2] + n // 2, [osb_t[:, :, P * n:P * n + P], ofx_t[:, :, P * n:P * n + P]])
            with sp.Fori(0, KT // 2) as n:
                for b in range(2):
                    load_w(b, USE_WO[b] + n, halves(wo_t, 2 * P * n + P * b))
            with sp.Fori(0, FF_CHUNKS) as ch:
                with sp.Fori(0, KT // 2) as n:
                    for b in range(2):
                        load_w(b, USE_FF[b] + KT * ch + n, halves(ff1_t, D * ch + 2 * P * n + P * b))
                with sp.Fori(0, KT // 2) as n:
                    for b in range(2):
                        col = 2 * P * n + P * b
                        load_w(b, USE_FF[b] + KT * ch + KT // 2 + n,
                               [ff2_t[:, bass.ds(KT * ch + 4 * hf, 4), bass.ds(col, P)] for hf in range(2)])
            for t in range(QB):
                sp.wait_ge(y_scaled[t % 2], t // 2 + 1)
                sp.dma_start(out_rows[t], y_nat[:, t, :]).then_inc(out_saved, 16)
            sp.wait_ge(out_saved, 16 * QB)

        @block.gpsimd
        def _(pool):
            for b in range(2):
                pool.sem_inc(w_split[b], START)
            nc.gpsimd.memset(ident[:, :], 0.0).then_inc(identity_made, 1)
            nc.gpsimd.memset(ident_b[:, :], 0.0).then_inc(identity_made, 1)
            for m in range(2):
                nc.gpsimd.memset(mask_b[m][:, :], 0.0).then_inc(identity_made, 1)
            nc.gpsimd.memset(ones[:, :], 1.0).then_inc(consts_made, 1)
            nc.gpsimd.memset(eps_col[:, :], EPS).then_inc(consts_made, 1)
            pool.wait_ge(identity_made, 4)
            for t in (ident, ident_b):
                nc.gpsimd.affine_select(out=t[:, :], in_=t[:, :], compare_op=ALU.not_equal, fill=1.0, base=0,
                                        pattern=[[-1, P]], channel_multiplier=1).then_inc(consts_made, 1)
            for m, op in enumerate((ALU.is_gt, ALU.is_ge)):
                nc.gpsimd.affine_select(out=mask_b[m][:, :], in_=mask_b[m][:, :], compare_op=op, fill=NEG, base=0,
                                        pattern=[[-1, P]], channel_multiplier=1).then_inc(consts_made, 1)

            def split(b, use):
                one = ones[:, :].unsqueeze(1).broadcast_to([P, 4, P])
                pool.wait_ge(w_loaded[b], 32 * use + 32)
                for hf in range(2):
                    raw = w_raw[b][:, 4 * hf:4 * hf + 4, :]
                    hi = w_hi[b][:, 4 * hf:4 * hf + 4, :]
                    lo = w_lo[b][:, 4 * hf:4 * hf + 4, :]
                    nc.gpsimd.tensor_tensor(hi, raw, one, ALU.mult).then_inc(hi_split[b], 1)
                    pool.wait_ge(hi_split[b], 2 * use + hf + 1)
                    nc.gpsimd.tensor_tensor(lo, raw, hi.bitcast(F32), ALU.subtract).then_inc(w_split[b], 1)

            pool.wait_ge(f_w_loaded, 16)
            pool.wait_ge(consts_made, 2)
            nc.gpsimd.tensor_tensor(w_f_hi[:, :, :], w_f_raw[:, :, :], ones[:, 0:HEADS].unsqueeze(1).broadcast_to([P, KT, HEADS]),
                                    ALU.mult).then_inc(f_w_split, 1)
            pool.wait_ge(f_w_split, 1)
            nc.gpsimd.tensor_tensor(w_f_lo[:, :, :], w_f_raw[:, :, :], w_f_hi[:, :, :].bitcast(F32),
                                    ALU.subtract).then_inc(f_w_split, 1)
            split(0, 0)
            split(1, 0)
            with pool.Fori(0, 2 * PAIRS) as G:
                done = DONE_F + DONE_ITER * G
                pool.wait_ge(dense_done, done + 2)
                split(0, 3 * G + 1)
                pool.wait_ge(dense_done, done + 4)
                split(1, 2 * G + 1)
                pool.wait_ge(dense_done, done + 6)
                split(0, 3 * G + 2)
                pool.wait_ge(gate_done, START + 4 * G + 2)
                split(1, 2 * G + 2)
                pool.wait_ge(gate_done, START + 4 * G + 4)
                split(0, 3 * G + 3)
            with pool.Fori(1, KT // 2) as n:
                for b in range(2):
                    pool.wait_ge(dense_done, DONE_MERGE - 4 + 4 * (2 * n + b))
                    split(b, USE_MERGE[b] + n)
            with pool.Fori(0, KT // 2) as n:
                for b in range(2):
                    pool.wait_ge(dense_done, DONE_WO - 2 + 2 * (2 * n + b))
                    split(b, USE_WO[b] + n)
            with pool.Fori(0, FF_CHUNKS * KT) as n:
                for b in range(2):
                    pool.wait_ge(dense_done, DONE_FF - 2 + 2 * (2 * n + b))
                    split(b, USE_FF[b] + n)

        @block.tensor
        def _(pe):
            pe.sem_inc(gate_done, START)
            pe.sem_inc(av_done, START)

            def three(dst, b, k, rhs, cols_, start, stop, w=None):
                hi, lo = w or (w_hi[b], w_lo[b])
                pe.matmul(dst, hi[:, k, :], rhs[0][:, k, cols_], start=start, stop=False)
                pe.matmul(dst, hi[:, k, :], rhs[1][:, k, cols_], start=False, stop=False)
                return pe.matmul(dst, lo[:, k, :], rhs[0][:, k, cols_], start=False, stop=stop)

            halves = [slice(0, HALF), slice(HALF, T)]

            def dense(b, use, rhs, bank, ready=None):
                for k in range(KT):
                    if k % 4 == 0:
                        pe.wait_ge(w_split[b], START + 2 * use + k // 4 + 1)
                    if ready is not None:
                        pe.wait_ge(*ready(k))
                    for hf in range(2):
                        mm = three(ps[:, bank + hf, :], b, k, rhs, halves[hf], k == 0, k == KT - 1)
                        if k == KT - 1:
                            mm.then_inc(dense_done, 1)

            def ada_total(m):
                pe.wait_ge(ada_used, KT * (m + 1))
                for n in range(KT):
                    mm = pe.matmul(ps[:, 6, n:n + 1], ada_sum[:, P * n:P * n + P], ones[:, 0:1], start=True, stop=True)
                mm.then_inc(ada_summed, 1)

            pe.wait_ge(consts_made, 6)
            pe.wait_ge(small_loaded, 16 * 9)
            pe.transpose(ps[:, 6, 0:PACK1], pack1[:, :], ident[0:PACK1, 0:PACK1])
            pe.transpose(ps[:, 6, PACK1:PACK1 + PACK2], pack2[:, :], ident[0:PACK2, 0:PACK2]).then_inc(pack_turned, 1)
            for t in range(QB):
                pe.wait_ge(x_loaded[t], 16)
                if t >= 2:
                    pe.wait_ge(x_kept_act, t - 1)
                    pe.wait_ge(x_kept_dve, t - 1)
                for k in range(KT):
                    mm = pe.transpose(ps[:, 2 * (t % 2) + k // 4, P * (k % 4):P * (k % 4) + P],
                                      x_in[:, t, P * k:P * k + P], ident[:, :])
                    if k % 4 == 3:
                        mm.then_inc(x_turned, 1)
            pe.wait_ge(diag_made, QB)
            for t in range(QB):
                mm = pe.matmul(ps[:, 4 + t // 4, P * (t % 4):P * (t % 4) + P], ones[:, :], diag[:, t, :], start=True, stop=True)
            mm.then_inc(rstd_spread, 1)
            pe.wait_ge(cols_made, 1)
            ada_total(0)
            pe.wait_ge(mod_made, 1)
            ada_total(1)
            pe.wait_ge(f_w_split, 2)
            for k in range(KT):
                pe.wait_ge(h_ready, k + 1)
                for hf in range(2):
                    mm = three(ps[0:HEADS, 2 + hf, :], None, k, h1, halves[hf], k == 0, k == KT - 1, (w_f_hi, w_f_lo))
                    if k == KT - 1:
                        mm.then_inc(dense_done, 1)

            def attend(G, fox):
                pe.wait_ge(scores_used, START + UNITS * G)
                dense(0, 3 * G, h1, 0)
                pe.wait_ge(dense_free, FREE_F + FREE_ITER * G)
                dense(1, 2 * G, h1, 2)
                pe.wait_ge(av_free, START + QB * G)
                pe.wait_ge(gate_copied, START + 4 * G)
                pe.wait_ge(mod_made, 2)
                dense(0, 3 * G + 1, h1, 6)

                def turn(idx, blocks, src):
                    if idx == 0:
                        pe.wait_ge(tp_free, START + TP_ITER * G)
                    else:
                        pe.wait_ge(tp_free, START + TP_ITER * G + idx - 1)
                    for n, blk in enumerate(blocks):
                        mm = pe.transpose(ps[:, 4 + idx % 2, P * n:P * n + P], src[:, P * blk:P * blk + P], ident[:, :])
                    mm.then_inc(tp_done, 1)

                def turn_values():
                    pe.wait_ge(v_copied, 2 * G + 2)
                    for idx in range(V_CHUNKS):
                        turn(idx, range(4 * idx, 4 * idx + 4), vT)

                def score(u):
                    h, i = divmod(u, QB)
                    if u < 2:
                        pe.wait_ge(dense_free, FREE_F + FREE_ITER * (G + 1))
                        if fox and u == 0:
                            pe.wait_ge(f_loaded, 64 * (G - PAIRS + 1))
                    else:
                        pe.wait_ge(scores_used, START + UNITS * G + u - 1)
                    n = P * (i + 1)
                    qs = slice(P * i, P * i + P)
                    for c0 in range(0, n, HALF):
                        ks = slice(c0, min(c0 + HALF, n))
                        dst = scores[u % 2][:, ks]
                        pe.matmul(dst, q_hi[h][:, qs], k_st[h][:, ks], start=True, stop=False)
                        if fox:
                            pe.matmul(dst, q_f[h][:, qs], k_f[h][:, ks], start=False, stop=False)
                        if c0 + HALF >= n:
                            pe.matmul(scores[u % 2][:, n - P:n], ident_b[:, :], mask_b[int(fox)][:, :],
                                      start=False, stop=False)
                        mm = pe.matmul(dst, q_lo[h][:, qs], k_st[h][:, ks], start=False, stop=True)
                    mm.then_inc(scores_ready, 1)

                def turn_probs(u):
                    pe.wait_ge(probs_ready, UNITS * G + u + 1)
                    i = u % QB
                    for n, idx in enumerate(chunks_of(u)):
                        turn(idx, range(4 * n, min(4 * n + 4, i + 1)), prob[:, u % 2, :])

                def values(u):
                    h, i = divmod(u, QB)
                    pe.wait_ge(tp_free, START + TP_ITER * G + chunks_of(u)[-1] + 1)
                    pe.wait_ge(av_free, START + QB * G + u // 2)
                    if u == 1 and not fox:
                        pe.wait_ge(mod_made, G + 3)
                    for kb in range(i + 1):
                        q0 = P if kb == i else 0
                        for s in range(2):
                            mm = pe.matmul(ps[:, 6, q0:2 * P], v_st[:, kb, h, :, :].rearrange("p a d -> p (a d)"),
                                           wT[s][:, kb, q0:2 * P], start=(kb == 0 and s == 0), stop=(kb == i and s == 1))
                    mm.then_inc(av_done, 1)

                def gate_step(s):
                    if not 0 <= s < UNITS:
                        return
                    tile, hf, quarter = s // 8, s // 4 % 2, s % 4
                    b = 1 - tile
                    use = 2 * G + 1 if tile == 0 else 3 * G + 2
                    if s == 0:
                        pe.wait_ge(v_copied, 2 * G + 2)
                    elif quarter == 0:
                        pe.wait_ge(gate_copied, START + 4 * G + s // 4)
                    if quarter % 2 == 0:
                        pe.wait_ge(w_split[b], START + 2 * use + quarter // 2 + 1)
                    for k in (2 * quarter, 2 * quarter + 1):
                        mm = three(ps[:, 7, :], b, k, h1, halves[hf], k == 0, k == KT - 1)
                    if k == KT - 1:
                        mm.then_inc(gate_done, 1)

                for s in range(STEPS):
                    if s < UNITS:
                        score(s)
                    if s == 1:
                        turn_values()
                    if s == 2 and not fox:
                        ada_total(G + 2)
                    if s >= 3 and s % 2 == 0:
                        values(s - 3)
                    if 2 <= s < UNITS + 2:
                        turn_probs(s - 2)
                    gate_step(s - GATE_LAG)

            with pe.Fori(0, PAIRS) as G:
                attend(G, False)
            with pe.Fori(PAIRS, 2 * PAIRS) as G:
                attend(G, True)

            pe.wait_ge(scores_used, START + 2 * PAIRS * UNITS)
            pe.wait_ge(tp_free, START + 2 * PAIRS * TP_ITER)
            pe.wait_ge(av_free, START + 2 * PAIRS * QB)
            pe.wait_ge(gate_copied, START + 8 * PAIRS)
            with pe.Fori(0, KT // 2) as n:
                for b in range(2):
                    pe.wait_ge(dense_free, FREE_MERGE - 2 + 2 * (2 * n + b))
                    for k in range(KT):
                        if k % 4 == 0:
                            pe.wait_ge(w_split[b], START + 2 * (USE_MERGE[b] + n) + k // 4 + 1)
                        pe.wait_ge(o_ready, k + 1)
                        for hf in range(2):
                            mm = three(ps[:, 4 * b + 2 * (k // 4) + hf, :], b, k, o_split, halves[hf],
                                       k % 4 == 0, k % 4 == 3)
                            if k % 4 == 3:
                                mm.then_inc(dense_done, 1)
            with pe.Fori(0, KT // 2) as n:
                for b in range(2):
                    pe.wait_ge(dense_free, FREE_WO - 2 + 2 * (2 * n + b))
                    dense(b, USE_WO[b] + n, merged, 2 * b, ready=lambda k: (dense_free, FREE_MERGE + 2 * k + 2))
            for hf in range(2):
                pe.wait_ge(sq_summed, 2 * KT - 1 + hf)
                pe.matmul(ps[:, 4 + hf, :], ones[:, :], ss_b[:, halves[hf]], start=True, stop=True).then_inc(stats_done, 1)
            for b in range(2):
                pe.wait_ge(dense_free, FREE_FF)
            for k in range(KT):
                pe.wait_ge(h_ready, KT + k + 1)
                for b in range(2):
                    if k % 4 == 0:
                        pe.wait_ge(w_split[b], START + 2 * USE_FF[b] + k // 4 + 1)
                    for hf in range(2):
                        mm = three(ps[:, 2 * b + hf, :], b, k, h2, halves[hf], k == 0, k == KT - 1)
                        if k == KT - 1:
                            mm.then_inc(dense_done, 1)

            def ff1_pair(ch, n):
                for b in range(2):
                    pe.wait_ge(dense_free, FREE_FF + 2 * KT * ch)
                    pe.wait_ge(act_free, KT - 2 + 2 * KT * ch + 2 * (2 * n + b))
                    dense(b, USE_FF[b] + KT * ch + n, h2, 2 * b)

            def ff2_tile(ch, n, b):
                pe.wait_ge(dense_free, FREE_FF - 2 + 2 * KT * ch + 2 * (2 * n + b))
                pe.wait_ge(act_free, KT + 2 * KT * ch + 14 + 2 * b)
                dense(b, USE_FF[b] + KT * ch + KT // 2 + n, hid, 2 * b,
                      ready=lambda k: (hid_ready, START + 2 * KT * ch + 2 * k + 2))

            with pe.Fori(1, KT // 2) as n:
                ff1_pair(0, n)
            with pe.Fori(0, KT // 2) as n:
                for b in range(2):
                    ff2_tile(0, n, b)
            with pe.Fori(1, FF_CHUNKS - 1) as ch:
                with pe.Fori(0, KT // 2) as n:
                    ff1_pair(ch, n)
                with pe.Fori(0, KT // 2) as n:
                    for b in range(2):
                        ff2_tile(ch, n, b)
            LAST = FF_CHUNKS - 1
            with pe.Fori(0, KT // 2) as n:
                ff1_pair(LAST, n)

            def turn_back(tile, b):
                pe.wait_ge(dense_free, FREE_LAST + 2 * tile + 2)
                pe.wait_ge(y_kept, START + 2 * tile - 2 * b)
                for t in range(QB):
                    mm = pe.transpose(ps[:, 4 + 2 * b + t // 4, P * (t % 4):P * (t % 4) + P],
                                      y_st[:, b, P * t:P * t + P], ident[:, :])
                    if t % 4 == 3:
                        mm.then_inc(y_turned, 1)

            def last_pair(n, first):
                ff2_tile(LAST, n, 0)
                if not first:
                    turn_back(2 * n - 1, 1)
                ff2_tile(LAST, n, 1)
                turn_back(2 * n, 0)

            last_pair(0, True)
            with pe.Fori(1, KT // 2) as n:
                last_pair(n, False)
            turn_back(KT - 1, 1)
            pe.wait_ge(sq_summed, 4 * KT)
            for t in range(QB):
                mm = pe.matmul(ps[:, 0, t:t + 1], ss_b[:, P * t:P * t + P], ones[:, 0:1], start=True, stop=True)
            mm.then_inc(stats_done, 1)

        @block.scalar
        def _(act):
            act.sem_inc(scores_used, START)
            act.sem_inc(gate_copied, START)
            for b in range(2):
                act.sem_inc(gate_saved[b], 16 * START)
            A = nc.scalar.activation
            halves = [slice(0, HALF), slice(HALF, T)]
            carrier = act.alloc_register("wait_carrier")
            carried = [0]

            def carry():
                carried[0] ^= 1
                act.reg_mov(carrier, carried[0])

            def norm_hi(which, k, tmp, h):
                act.wait_ge(normed, KT * which + k + 1)
                A(h[0][:, k, :], tmp, ACT.Identity,
                  bias=mod[:, 3 * KT * which + k:3 * KT * which + k + 1]).then_inc(h_hi, 1)

            act.wait_ge(consts_made, 6)
            for t in range(QB):
                act.wait_ge(x_loaded[t], 16)
                if t >= 2:
                    act.wait_ge(x_squared, t - 1)
                A(sq_a[:, t % 2, :], x_in[:, t, :], ACT.Square, accum_out=rms_a[:, t:t + 1]).then_inc(x_squared, 1)
                act.wait_ge(x_turned, 2 * t + 1)
                A(xT[:, 0:KT // 2, P * t:P * t + P], ps[:, 2 * (t % 2), :].rearrange("p (k t) -> p k t", t=P),
                  ACT.Copy).then_inc(x_kept_act, 1)
            act.wait_ge(x_squared, QB)
            A(rms_a[:, :], rms_a[:, :], ACT.Sqrt, bias=eps_col[:, 0:1], scale=1.0 / D).then_inc(root_done, 1)
            act.wait_ge(mod_made, 2)
            for k in range(KT):
                norm_hi(0, k, x_scaled[:, k, :], h1)
            act.wait_ge(x_kept_act, QB)
            act.wait_ge(x_kept_dve, QB)
            act.dma_start(xT_dram.rearrange("k p t -> p k t"), xT[:, :, :]).then_inc(x_saved, 16)
            act.wait_ge(dense_done, DONE_F)
            A(f_abs[:, :], ps[0:HEADS, 2:4, :].rearrange("p a b -> p (a b)"), ACT.Abs,
              bias=bf_col[:, 0:1]).then_inc(f_step_act, 1)
            act.wait_ge(f_step_act, 1)
            A(f_abs[:, :], f_abs[:, :], ACT.Exp, scale=-1.0).then_inc(f_step_act, 1)
            act.wait_ge(f_step_act, 2)
            A(f_abs[:, :], f_abs[:, :], ACT.Ln, bias=ones[0:HEADS, 0:1]).then_inc(f_step_act, 1)
            act.wait_ge(f_step_dve, 8)
            act.dma_start(fparts_dram, f_parts[:, :, :]).then_inc(f_stored, 16)

            def attend(G, fox):
                done = DONE_F + DONE_ITER * G
                for hf in range(2):
                    act.wait_ge(dense_done, done + hf + 1)
                    A(k_st[0][0:DH, halves[hf]], ps[0:DH, hf, :], ACT.Copy)
                    A(k_st[1][DH:P, halves[hf]], ps[DH:P, hf, :], ACT.Copy).then_inc(k_hi_done, 1)
                for hf in range(2):
                    act.wait_ge(dense_done, done + 2 + hf + 1)
                    for h in range(2):
                        rows = slice(DH * h, DH * h + DH)
                        for to in range(2):
                            last = A(q_hi[h][DH * to:DH * to + DH, halves[hf]], ps[rows, 2 + hf, :], ACT.Copy, scale=SCALE)
                    last.then_inc(q_hi_done, 1)
                for hf in range(2):
                    act.wait_ge(dense_done, done + 4 + hf + 1)
                    act.wait_ge(gate_saved[hf], 16 * START + 32 * G)
                    A(vT[:, halves[hf]], ps[:, 6 + hf, :], ACT.Copy).then_inc(v_copied, 1)

                def values_hi():
                    for idx in range(V_CHUNKS):
                        act.wait_ge(tp_done, TP_ITER * G + idx + 1)
                        A(v_st[:, 4 * idx:4 * idx + 4, :, 0, :],
                          ps[:, 4 + idx, :].rearrange("p (b h d) -> p b h d", h=2, d=DH), ACT.Copy).then_inc(tp_hi, 1)

                def gate_out(q):
                    act.wait_ge(gate_done, START + 4 * G + q + 1)
                    act.wait_ge(gate_saved[q % 2], 16 * START + 16 * (2 * G + q // 2))
                    A(gate_st[:, q % 2, :], ps[:, 7, :], ACT.Copy).then_inc(gate_copied, 1)

                def gate_store(q):
                    act.wait_ge(gate_copied, START + 4 * G + q + 1)
                    act.dma_start(gates_dram[bass.ds(2 * G + q // 2, 1), :, halves[q % 2]].rearrange("a p t -> (a p) t"),
                                  gate_st[:, q % 2, :]).then_inc(gate_saved[q % 2], 16)

                def fold_values(u):
                    h = u // QB
                    own, other = slice(DH * h, DH * h + DH), slice(DH * (1 - h), DH * (1 - h) + DH)
                    act.wait_ge(av_done, START + QB * G + u // 2 + 1)
                    act.wait_ge(av_free, START + QB * G + u // 2)
                    A(fold[own, :], ps[other, 6, 0:2 * P], ACT.Copy).then_inc(av_folded, 1)

                def weights_hi(u):
                    i = u % QB
                    if i % 2 == 0:
                        act.wait_ge(av_done, START + QB * G + u // 2)
                    q0 = P * (i % 2)
                    for n, idx in enumerate(chunks_of(u)):
                        nb = min(4, i + 1 - 4 * n)
                        act.wait_ge(tp_done, TP_ITER * G + idx + 1)
                        A(wT[0][:, 4 * n:4 * n + nb, q0:q0 + P],
                          ps[:, 4 + idx % 2, 0:P * nb].rearrange("p (b q) -> p b q", q=P), ACT.Copy).then_inc(tp_hi, 1)

                def scores_out(u):
                    n = P * (u % QB + 1)
                    act.wait_ge(scores_ready, UNITS * G + u + 1)
                    if u >= 2:
                        act.wait_ge(tp_done, TP_ITER * G + chunks_of(u - 2)[-1] + 1)
                    z = scores[u % 2][:, 0:n]
                    if fox:
                        act.wait_ge(max_ready, UNITS * (G - PAIRS) + u + 1)
                        A(prob[:, u % 2, 0:n], z, ACT.Exp, bias=neg_max[:, u % 2:u % 2 + 1],
                          accum_out=row_sum[:, u % 2:u % 2 + 1]).then_inc(scores_used, 1)
                    else:
                        A(prob[:, u % 2, 0:n], z, ACT.Sigmoid)
                        A(surv[:, u % 2, 0:n], z, ACT.Sigmoid, scale=-1.0).then_inc(scores_used, 1)

                for s in range(STEPS):
                    q, at_q = divmod(s - GATE_LAG, 4)
                    if q >= 1 and at_q == 1:
                        gate_store(q - 1)
                    if q >= 1 and at_q == 0:
                        gate_out(q - 1)
                    if s == 1:
                        values_hi()
                    if s >= 3 and s % 2 == 0:
                        fold_values(s - 3)
                    if 2 <= s < UNITS + 2:
                        weights_hi(s - 2)
                    if s < UNITS:
                        scores_out(s)

            with act.Fori(0, PAIRS) as G:
                attend(G, False)
            with act.Fori(PAIRS, 2 * PAIRS) as G:
                attend(G, True)

            act.wait_ge(gate_done, START + 8 * PAIRS)
            act.wait_ge(av_free, START + 2 * PAIRS * QB)
            for k in range(KT):
                A(o_split[0][:, k, :], mixed[:, k, :], ACT.Copy).then_inc(o_hi_done, 1)
            for b in range(2):
                act.wait_ge(gate_saved[b], 16 * START + 16 * 4 * 2 * PAIRS // 2)

            both_mixers = gates_dram.rearrange("(m k) p t -> k p m t", m=2)

            def gates_back(tile, b):
                act.dma_start(gates[:, b, :, :], both_mixers[bass.ds(tile, 1)].rearrange("a p m t -> (a p) m t")
                              ).then_inc(gate_back[b], 16)

            def merge_pair(n, last):
                for b in range(2):
                    act.wait_ge(gate_back[b], 16 * n + 16)
                    carry()
                    for m in range(2):
                        A(gates[:, b, m, :], gates[:, b, m, :], ACT.Sigmoid,
                          bias=cols[:, bass.ds(COL_BGATE + KT * m + 2 * n + b, 1)]).then_inc(gate_on, 1)
                    if not (last and b == 1):
                        act.wait_ge(dense_free, FREE_MERGE + 2 * (2 * n + b))
                        if b == 0:
                            gates_back(2 * n + 1, 1)
                        else:
                            gates_back(2 * n + 2, 0)
                    for hf in range(2):
                        act.wait_ge(merge_sum, 4 * n + 2 * b + hf + 1)
                        carry()
                        A(merged[0][:, bass.ds(2 * n + b, 1), halves[hf]].rearrange("p a t -> p (a t)"),
                          gates[:, b, 0, halves[hf]], ACT.Copy).then_inc(merge_hi, 1)

            act.wait_ge(dense_free, FREE_MERGE)
            gates_back(0, 0)
            with act.Fori(0, KT // 2 - 1) as n:
                merge_pair(n, False)
            merge_pair(KT // 2 - 1, True)
            def square(n):
                if n >= 2:
                    act.wait_ge(sq_summed, n - 1)
                A(sq_b[:, n % 2, :], res[:, n // 2, halves[n % 2]], ACT.Square).then_inc(squared, 1)

            act.wait_ge(x_saved, 16)
            for k in range(KT):
                for hf in range(2):
                    act.wait_ge(dense_free, FREE_WO - 1 + 2 * k + hf if k else FREE_WO)
                    act.dma_start(x_again[:, hf, :], xT_dram[k, :, halves[hf]]).then_inc(x_back[hf], 16)
                if k:
                    for hf in range(2):
                        square(2 * (k - 1) + hf)
            for hf in range(2):
                act.wait_ge(dense_free, FREE_WO + 2 * (KT - 1) + hf + 1)
                square(2 * (KT - 1) + hf)
            for hf in range(2):
                act.wait_ge(stats_done, hf + 1)
                A(rstd_b[:, halves[hf]], ps[:, 4 + hf, :], ACT.Sqrt, bias=eps_col[:, 0:1], scale=1.0 / D).then_inc(root_done, 1)
            for k in range(KT):
                norm_hi(1, k, norm_b[:, k % 2, :], h2)
                A(res[:, k, :], res[:, k, :], ACT.Identity, bias=gt_b[:, k:k + 1]).then_inc(act_free, 1)
            with act.Fori(0, FF_CHUNKS) as ch:
                with act.Fori(0, KT) as n:
                    for hf in range(2):
                        act.wait_ge(dense_done, DONE_FF + 4 * KT * ch + 2 * n + hf + 1)
                        act.wait_ge(hid_ready, START + 2 * KT * ch + 2 * n + hf)
                        carry()
                        A(relu[:, hf, :], ps[:, bass.ds(2 * (n % 2) + hf, 1), :].rearrange("p a t -> p (a t)"), ACT.Relu,
                          bias=cols[:, bass.ds(COL_BFF1 + KT * ch + n, 1)]).then_inc(act_free, 1)
                        act.wait_ge(act_free, KT + 2 * KT * ch + 2 * n + hf + 1)
                        carry()
                        A(hid[0][:, bass.ds(n, 1), halves[hf]].rearrange("p a t -> p (a t)"), relu[:, hf, :],
                          ACT.Square).then_inc(hid_hi, 1)
            act.wait_ge(dense_done, DONE_FF + 4 * KT * (FF_CHUNKS - 1) + 2 * KT)
            act.dma_start(gain_row[:, :], g_final.rearrange("(l d) -> l d", l=1).partition_broadcast(P)
                          ).then_inc(gain_loaded, 16)
            with act.Fori(0, KT // 2) as n:
                for b in range(2):
                    for hf in range(2):
                        act.wait_ge(dense_free, FREE_LAST + 4 * n + 2 * b + hf + 1)
                        act.wait_ge(sq_summed, 2 * KT + 4 * n + 2 * b + hf - 1)
                        A(sq_b[:, hf, :], y_st[:, b, halves[hf]], ACT.Square).then_inc(squared, 1)
            act.wait_ge(stats_done, 3)
            A(rms_c[:, :], ps[:, 0, 0:QB], ACT.Sqrt, bias=eps_col[:, 0:1], scale=1.0 / D).then_inc(root_done, 1)
            act.wait_ge(rstd_made, 4)
            act.wait_ge(y_kept, START + 2 * KT)
            for t in range(1, QB, 2):
                A(y_nat[:, t, :], y_nat[:, t, :], ACT.Copy, scale=rstd_c[:, t:t + 1]).then_inc(y_scaled[1], 1)

        @block.vector
        def _(dve):
            dve.sem_inc(av_free, START)
            dve.sem_inc(tp_free, START)
            dve.sem_inc(hid_ready, START)
            dve.sem_inc(y_kept, START)
            V = nc.vector
            halves = [slice(0, HALF), slice(HALF, T)]

            def ada_add(order, k, tile):
                ck = cols[:, COL_C + k:COL_C + k + 1]
                if k == 0:
                    V.tensor_scalar(ada_sum[:, :], tile, ck, None, ALU.mult).then_inc(ada_used, 1)
                else:
                    dve.wait_ge(ada_used, KT * order + k)
                    V.scalar_tensor_tensor(out=ada_sum[:, :], in0=tile, scalar=ck, in1=ada_sum[:, :],
                                           op0=ALU.mult, op1=ALU.add).then_inc(ada_used, 1)

            def ada_step(m, k):
                dve.wait_ge(ada_loaded[k % 2], 16 * (KT // 2 * (m - 2) + k // 2) + 16)
                if k == 0:
                    dve.wait_ge(ada_summed, m)
                ada_add(m, k, ada[:, k % 2, :])

            def mod_cols(m, order=None):
                dve.wait_ge(ada_summed, (m if order is None else order) + 1)
                V.tensor_tensor(mod[:, bass.ds(KT * m, KT)], ps[:, 6, 0:KT], cols[:, bass.ds(COL_BADA + KT * m, KT)],
                                ALU.add).then_inc(mod_made, 1)

            def add_square(n):
                dve.wait_ge(squared, n + 1)
                half = ss_b[:, halves[n % 2]]
                if n < 2:
                    ins = V.tensor_copy(half, sq_b[:, n % 2, :])
                else:
                    dve.wait_ge(sq_summed, n - 1)
                    ins = V.tensor_tensor(half, half, sq_b[:, n % 2, :], ALU.add)
                ins.then_inc(sq_summed, 1)

            def rest(which, k, tmp, h):
                dve.wait_ge(h_hi, KT * which + k + 1)
                V.scalar_tensor_tensor(out=h[1][:, k, :], in0=tmp, scalar=mod[:, 3 * KT * which + k:3 * KT * which + k + 1],
                                       in1=h[0][:, k, :].bitcast(F32), op0=ALU.add, op1=ALU.subtract).then_inc(h_ready, 1)

            dve.wait_ge(pack_turned, 1)
            V.tensor_copy(cols[:, :], ps[:, 6, 0:PACK1 + PACK2]).then_inc(cols_made, 1)
            for t in range(QB):
                dve.wait_ge(x_turned, 2 * t + 2)
                V.tensor_copy(xT[:, KT // 2:KT, P * t:P * t + P], ps[:, 2 * (t % 2) + 1, :].rearrange("p (k t) -> p k t", t=P)
                              ).then_inc(x_kept_dve, 1)
            dve.wait_ge(cols_made, 1)
            dve.wait_ge(root_done, 1)
            V.reciprocal(rstd_a[:, :], rms_a[:, :]).then_inc(rstd_made, 1)
            dve.wait_ge(rstd_made, 1)
            for t in range(QB):
                V.tensor_scalar(diag[:, t, :], ident[:, :], rstd_a[:, t:t + 1], None, ALU.mult).then_inc(diag_made, 1)
            for k in range(KT):
                dve.wait_ge(ada_in[k // 2], 16)
                ada_add(0, k, ada_first[:, k, :])
            mod_cols(1, order=0)
            dve.wait_ge(mod_made, 1)
            V.scalar_tensor_tensor(out=g_sc[0][:, :], in0=mod[:, KT:2 * KT], scalar=1.0, in1=cols[:, COL_GMIX:COL_GMIX + KT],
                                   op0=ALU.add, op1=ALU.mult).then_inc(mod_derived, 1)
            dve.wait_ge(mod_derived, 1)
            dve.wait_ge(rstd_spread, 1)
            dve.wait_ge(x_kept_act, QB)
            spread = ps[:, 4:6, :].rearrange("p a b -> p (a b)")
            for k in range(KT):
                dve.wait_ge(ada_in[KT // 2 + k // 2], 16)
                ada_add(1, k, ada_first[:, KT + k, :])
                V.scalar_tensor_tensor(out=x_scaled[:, k, :], in0=xT[:, k, :], scalar=g_sc[0][:, k:k + 1], in1=spread,
                                       op0=ALU.mult, op1=ALU.mult).then_inc(normed, 1)
            mod_cols(0, order=1)
            dve.wait_ge(mod_made, 2)
            for k in range(KT):
                rest(0, k, x_scaled[:, k, :], h1)

            fl = ps[0:HEADS, 2:4, :].rearrange("p a b -> p (a b)")
            dve.wait_ge(f_step_act, 1)
            V.tensor_scalar(f_log[:, 0:HALF], fl[:, 0:HALF], bf_col[:, 0:1], 0.0, ALU.add, ALU.min).then_inc(dense_free, 1)
            V.tensor_scalar(f_log[:, HALF:T], fl[:, HALF:T], bf_col[:, 0:1], 0.0, ALU.add, ALU.min).then_inc(dense_free, 1)
            dve.wait_ge(dense_free, FREE_F)
            dve.wait_ge(f_step_act, 3)
            V.tensor_tensor(f_log[:, :], f_log[:, :], f_abs[:, :], ALU.subtract).then_inc(f_step_dve, 1)
            dve.wait_ge(f_step_dve, 1)
            V.tensor_tensor_scan(f_cum[:, :], f_log[:, :], ones[0:HEADS, 0:1].to_broadcast([HEADS, T]), 0.0,
                                 ALU.add, ALU.mult).then_inc(f_step_dve, 1)
            dve.wait_ge(f_step_dve, 2)
            part = f_cum
            for n in range(3):
                V.tensor_copy(f_parts[:, n, :], part[:, :]).then_inc(f_step_dve, 1)
                dve.wait_ge(f_step_dve, 3 + 2 * n)
                V.tensor_tensor(f_rest[:, :], part[:, :], f_parts[:, n, :], ALU.subtract).then_inc(f_step_dve, 1)
                dve.wait_ge(f_step_dve, 4 + 2 * n)
                part = f_rest

            def attend(G, fox):
                if not fox:
                    for k in range(4):
                        ada_step(G + 2, k)
                for hf in range(2):
                    dve.wait_ge(k_hi_done, 2 * G + hf + 1)
                    for h in range(2):
                        own, other = slice(DH * h, DH * h + DH), slice(DH * (1 - h), DH * (1 - h) + DH)
                        last = V.tensor_tensor(k_st[h][other, halves[hf]], ps[own, hf, :],
                                               k_st[h][own, halves[hf]].bitcast(F32), ALU.subtract)
                    last.then_inc(dense_free, 1)
                for hf in range(2):
                    dve.wait_ge(q_hi_done, 2 * G + hf + 1)
                    for h in range(2):
                        own = slice(DH * h, DH * h + DH)
                        for to in range(2):
                            last = V.scalar_tensor_tensor(
                                out=q_lo[h][DH * to:DH * to + DH, halves[hf]], in0=ps[own, 2 + hf, :], scalar=SCALE,
                                in1=q_hi[h][own, halves[hf]].bitcast(F32), op0=ALU.mult, op1=ALU.subtract)
                    last.then_inc(dense_free, 1)
                if not fox:
                    for k in range(4, KT):
                        ada_step(G + 2, k)

                def values_lo():
                    for idx in range(V_CHUNKS):
                        dve.wait_ge(tp_hi, TP_ITER * G + idx + 1)
                        V.tensor_tensor(v_st[:, 4 * idx:4 * idx + 4, :, 1, :],
                                        ps[:, 4 + idx, :].rearrange("p (b h d) -> p b h d", h=2, d=DH),
                                        v_st[:, 4 * idx:4 * idx + 4, :, 0, :].bitcast(F32), ALU.subtract).then_inc(tp_free, 1)
                    if not fox:
                        dve.wait_ge(f_stored, 16)
                        dve.wait_ge(x_saved, 16)

                def add_values(u):
                    h, i = divmod(u, QB)
                    own = slice(DH * h, DH * h + DH)
                    dve.wait_ge(av_folded, QB * G + u // 2 + 1)
                    q0 = P * (i - 1)
                    V.tensor_tensor(mixed[own, bass.ds(G, 1), q0:q0 + 2 * P].rearrange("p a t -> p (a t)"),
                                    ps[own, 6, 0:2 * P], fold[own, :], ALU.add).then_inc(av_free, 1)

                def weights_lo(u):
                    i = u % QB
                    q0 = P * (i % 2)
                    for n, idx in enumerate(chunks_of(u)):
                        nb = min(4, i + 1 - 4 * n)
                        dve.wait_ge(tp_hi, TP_ITER * G + idx + 1)
                        V.tensor_tensor(wT[1][:, 4 * n:4 * n + nb, q0:q0 + P],
                                        ps[:, 4 + idx % 2, 0:P * nb].rearrange("p (b q) -> p b q", q=P),
                                        wT[0][:, 4 * n:4 * n + nb, q0:q0 + P].bitcast(F32),
                                        ALU.subtract).then_inc(tp_free, 1)

                def row_max(u):
                    n = P * (u % QB + 1)
                    dve.wait_ge(scores_ready, UNITS * G + u + 1)
                    V.tensor_reduce(neg_max[:, u % 2:u % 2 + 1], scores[u % 2][:, 0:n], AX.X, ALU.max,
                                    negate=True).then_inc(max_ready, 1)

                def finish_weights(u):
                    n = P * (u % QB + 1)
                    dve.wait_ge(scores_used, START + UNITS * G + u + 1)
                    pr = prob[:, u % 2, 0:n]
                    if fox:
                        V.reciprocal(inv_sum[:, u % 2:u % 2 + 1], row_sum[:, u % 2:u % 2 + 1]).then_inc(inv_ready, 1)
                        dve.wait_ge(inv_ready, UNITS * (G - PAIRS) + u + 1)
                        V.tensor_scalar(pr, pr, inv_sum[:, u % 2:u % 2 + 1], None, ALU.mult).then_inc(probs_ready, 1)
                    else:
                        sv = surv[:, u % 2, 0:n]
                        V.tensor_tensor_scan(sv[:, ::-1], sv[:, ::-1], ones[:, 0:1].to_broadcast([P, n]), 1.0, ALU.mult,
                                             ALU.mult).then_inc(scanned, 1)
                        dve.wait_ge(scanned, UNITS * G + u + 1)
                        V.tensor_tensor(pr[:, 0:n - 1], pr[:, 0:n - 1], sv[:, 1:n], ALU.mult).then_inc(probs_ready, 1)

                for s in range(STEPS):
                    if fox and s < UNITS:
                        row_max(s)
                    if s == 1:
                        values_lo()
                    if s == 2 and not fox:
                        mod_cols(G + 2)
                    if s >= 3 and s % 2 == 0:
                        add_values(s - 3)
                    if 2 <= s < UNITS + 2:
                        weights_lo(s - 2)
                    if s < UNITS:
                        finish_weights(s)

            with dve.Fori(0, PAIRS) as G:
                attend(G, False)
            dve.wait_ge(mod_made, N_MOD)
            for h in range(2):
                V.memset(q_f[h][:, :], -1.0).then_inc(f_ones, 1)
                V.memset(k_f[h][:, :], 1.0).then_inc(f_ones, 1)
            V.scalar_tensor_tensor(out=g_sc[1][:, :], in0=mod[:, 4 * KT:5 * KT], scalar=1.0, in1=cols[:, COL_GMLP:COL_GMLP + KT],
                                   op0=ALU.add, op1=ALU.mult).then_inc(mod_derived, 1)
            V.tensor_tensor(gt_b[:, :], mod[:, 5 * KT:6 * KT], cols[:, COL_BFF2:COL_BFF2 + KT], ALU.mult).then_inc(mod_derived, 1)
            dve.wait_ge(mod_derived, 3)
            with dve.Fori(PAIRS, 2 * PAIRS) as G:
                attend(G, True)

            for k in range(KT):
                dve.wait_ge(o_hi_done, k + 1)
                V.tensor_tensor(o_split[1][:, k, :], mixed[:, k, :], o_split[0][:, k, :].bitcast(F32),
                                ALU.subtract).then_inc(o_ready, 1)
            with dve.Fori(0, KT // 2) as n:
                for b in range(2):
                    for hf in range(2):
                        step = 4 * n + 2 * b + hf
                        sb, fox = (gates[:, b, m, halves[hf]] for m in range(2))
                        for m, g in enumerate((sb, fox)):
                            dve.wait_ge(gate_on, 4 * n + 2 * b + m + 1)
                            dve.wait_ge(dense_done, DONE_MERGE + 8 * n + 4 * b + 2 * m + hf + 1)
                            V.tensor_tensor(g, ps[:, 4 * b + 2 * m + hf, :], g, ALU.mult).then_inc(merge_mul, 1)
                        dve.wait_ge(merge_mul, 2 * step + 2)
                        V.tensor_tensor(sb, sb, fox, ALU.add).then_inc(merge_sum, 1)
                        dve.wait_ge(merge_hi, step + 1)
                        V.tensor_tensor(merged[1][:, bass.ds(2 * n + b, 1), halves[hf]].rearrange("p a t -> p (a t)"), sb,
                                        merged[0][:, bass.ds(2 * n + b, 1), halves[hf]].rearrange("p a t -> p (a t)").bitcast(F32),
                                        ALU.subtract).then_inc(dense_free, 1)
            for k in range(KT):
                for hf in range(2):
                    dve.wait_ge(dense_done, DONE_WO + 2 * k + hf + 1)
                    dve.wait_ge(x_back[hf], 16 * k + 16)
                    V.scalar_tensor_tensor(out=res[:, k, halves[hf]], in0=ps[:, 2 * (k % 2) + hf, :],
                                           scalar=mod[:, 2 * KT + k:2 * KT + k + 1], in1=x_again[:, hf, :],
                                           op0=ALU.mult, op1=ALU.add).then_inc(dense_free, 1)
                if k:
                    add_square(2 * k - 2)
                    add_square(2 * k - 1)
            add_square(2 * KT - 2)
            add_square(2 * KT - 1)
            for hf in range(2):
                dve.wait_ge(root_done, 2 + hf)
                V.reciprocal(rstd_b[:, halves[hf]], rstd_b[:, halves[hf]]).then_inc(rstd_made, 1)
            dve.wait_ge(rstd_made, 3)
            for k in range(KT):
                if k >= 2:
                    dve.wait_ge(h_ready, KT + k - 1)
                V.scalar_tensor_tensor(out=norm_b[:, k % 2, :], in0=res[:, k, :], scalar=g_sc[1][:, k:k + 1],
                                       in1=rstd_b[:, :], op0=ALU.mult, op1=ALU.mult).then_inc(normed, 1)
                if k:
                    rest(1, k - 1, norm_b[:, (k - 1) % 2, :], h2)
            rest(1, KT - 1, norm_b[:, (KT - 1) % 2, :], h2)
            dve.wait_ge(act_free, KT)
            def hidden(ch):
                with dve.Fori(0, KT) as n:
                    for hf in range(2):
                        step = 2 * KT * ch + 2 * n + hf
                        dve.wait_ge(act_free, KT + step + 1)
                        V.tensor_tensor(relu_sq[:, hf, :], relu[:, hf, :], relu[:, hf, :], ALU.mult).then_inc(relu_squared, 1)
                        dve.wait_ge(relu_squared, step + 1)
                        dve.wait_ge(hid_hi, step + 1)
                        V.tensor_tensor(hid[1][:, bass.ds(n, 1), halves[hf]].rearrange("p a t -> p (a t)"), relu_sq[:, hf, :],
                                        hid[0][:, bass.ds(n, 1), halves[hf]].rearrange("p a t -> p (a t)").bitcast(F32),
                                        ALU.subtract).then_inc(hid_ready, 1)

            def residual(ch, n, b, out_tile=None):
                for hf in range(2):
                    step = 2 * KT * ch + 4 * n + 2 * b + hf
                    dve.wait_ge(dense_done, DONE_FF + 4 * KT * ch + 2 * KT + 4 * n + 2 * b + hf + 1)
                    dve.wait_ge(dense_free, FREE_FF - 2 * KT + step + 1)
                    tile = res[:, bass.ds(2 * n + b, 1), halves[hf]].rearrange("p a t -> p (a t)")
                    V.scalar_tensor_tensor(out=tile if out_tile is None else out_tile[:, halves[hf]], in0=ps[:, 2 * b + hf, :],
                                           scalar=mod[:, bass.ds(5 * KT + 2 * n + b, 1)], in1=tile,
                                           op0=ALU.mult, op1=ALU.add).then_inc(dense_free, 1)

            with dve.Fori(0, FF_CHUNKS - 1) as ch:
                hidden(ch)
                with dve.Fori(0, KT // 2) as n:
                    for b in range(2):
                        residual(ch, n, b)
            hidden(FF_CHUNKS - 1)
            dve.wait_ge(gain_loaded, 16)

            def sum_squares(tile, first=False):
                for hf in range(2):
                    n = 2 * tile + hf
                    dve.wait_ge(squared, 2 * KT + n + 1)
                    dve.wait_ge(sq_summed, 2 * KT + n - 1)
                    half = ss_b[:, halves[hf]]
                    if first:
                        V.tensor_copy(half, sq_b[:, hf, :]).then_inc(sq_summed, 1)
                    else:
                        V.tensor_tensor(half, half, sq_b[:, hf, :], ALU.add).then_inc(sq_summed, 1)

            def keep(tile, b):
                for hf in range(2):
                    dve.wait_ge(y_turned, 2 * tile + hf + 1)
                    V.tensor_tensor(y_nat[:, 4 * hf:4 * hf + 4, bass.ds(P * tile, P)],
                                    ps[:, 4 + 2 * b + hf, :].rearrange("p (t d) -> p t d", d=P),
                                    gain_row[:, bass.ds(P * tile, P)].unsqueeze(1).broadcast_to([P, 4, P]),
                                    ALU.mult).then_inc(y_kept, 1)

            def last_pair(n, first):
                residual(FF_CHUNKS - 1, n, 0, y_st[:, 0, :])
                if not first:
                    sum_squares(2 * n - 1)
                    keep(2 * n - 1, 1)
                residual(FF_CHUNKS - 1, n, 1, y_st[:, 1, :])
                sum_squares(2 * n, first)
                keep(2 * n, 0)

            last_pair(0, True)
            with dve.Fori(1, KT // 2) as n:
                last_pair(n, False)
            sum_squares(KT - 1)
            keep(KT - 1, 1)
            dve.wait_ge(root_done, 4)
            V.reciprocal(rstd_c[:, :], rms_c[:, :]).then_inc(rstd_made, 1)
            dve.wait_ge(rstd_made, 4)
            dve.wait_ge(y_kept, START + 2 * KT)
            for t in range(0, QB, 2):
                V.tensor_scalar(y_nat[:, t, :], y_nat[:, t, :], rstd_c[:, t:t + 1], None, ALU.mult).then_inc(y_scaled[0], 1)


_INS = ["x", "c", "w_ada", "b_ada", "g_mix", "w_in", "b_f", "w_gate", "b_gate", "w_out_sb", "w_out_fox",
        "w_o", "g_mlp", "w_ff1", "b_ff1", "w_ff2", "b_ff2", "g_final"]


def kernel(**inputs):
    import numpy as np
    import concourse.bacc as bacc
    from concourse.bass_utils import run_bass_kernel_spmd

    nc = bacc.Bacc("TRN2", target_bir_lowering=False, num_devices=1)
    arrays, args = {}, []
    for name in _INS:
        a = np.ascontiguousarray(inputs[name])
        arrays[f"in_{name}"] = a
        args.append(nc.dram_tensor(f"in_{name}", a.shape, mybir.dt.from_np(a.dtype), kind="ExternalInput").ap())
    shape = inputs["x"].shape
    args.append(nc.dram_tensor("out_0", shape, F32, kind="ExternalOutput").ap())
    build_block(nc, *args)
    r = run_bass_kernel_spmd(nc, [arrays], core_ids=[0])
    return r.results[0]["out_0"]
```

```python
from contextlib import ExitStack

import concourse.bass as bass
from concourse import mybir

P = 128
D = 1024
T = 1024
KT = D // P
HALF = 512
HEADS = 8
DH = 64
D_MIX = HEADS * DH
N_MOD = 6
QB = T // P
PAIRS = HEADS // 2
UNITS = 2 * QB
EPS = 1e-6
SCALE = DH ** -0.5
NEG = -1.0e30
FF_CHUNKS = 4

F32 = mybir.dt.float32
F32R = mybir.dt.float32r
BF16 = mybir.dt.bfloat16
ALU = mybir.AluOpType
ACT = mybir.ActivationFunctionType
AX = mybir.AxisListType

COL_GMIX, COL_GMLP, COL_BGATE, COL_BFF1, COL_C, COL_BFF2, COL_BADA = 0, 8, 16, 32, 64, 72, 80
PACK1 = COL_BADA
PACK2 = N_MOD * KT

DONE_F, DONE_ITER = 2, 6
DONE_MERGE = DONE_F + 2 * PAIRS * DONE_ITER
DONE_WO = DONE_MERGE + 4 * KT
DONE_FF = DONE_WO + 2 * KT
FREE_F, FREE_ITER = 2, 4
FREE_MERGE = FREE_F + 2 * PAIRS * FREE_ITER
FREE_WO = FREE_MERGE + 2 * KT
FREE_FF = FREE_WO + 2 * KT
FREE_LAST = FREE_FF + 2 * KT * (FF_CHUNKS - 1)
ADA_FIRST = KT + KT // 2 + 1
START = 1
USE_MERGE = (2 * 2 * PAIRS, 3 * 2 * PAIRS)
USE_WO = (USE_MERGE[0] + KT // 2, USE_MERGE[1] + KT // 2)
USE_FF = (USE_WO[0] + KT // 2, USE_WO[1] + KT // 2)
V_CHUNKS = 2


def chunks_of(u):
    first = V_CHUNKS
    for w in range(u):
        first += 1 if w % QB < 4 else 2
    return list(range(first, first + (1 if u % QB < 4 else 2)))


TP_ITER = chunks_of(UNITS - 1)[-1] + 1
SCALED_BY_ACT = ((1, 3), (7,))
OUT_ORDER = (0, 1, 2, 3, 4, 7, 5, 6)
GATES_FIRST = (8, 10, 16, 17)
GATE_STEPS = (1, 2, 3, 4, 5, 6, 7, 8, 10, 11, 12, 13, 14, 15, 16, 17)
STEPS = UNITS + 3


def build_block(nc, x, c, w_ada, b_ada, g_mix, w_in, b_f, w_gate, b_gate, w_out_sb, w_out_fox,
                w_o, g_mlp, w_ff1, b_ff1, w_ff2, b_ff2, g_final, out):
    x_rows = x.rearrange("b (t p) d -> (b t) p d", p=P)
    out_rows = out.rearrange("b (t p) d -> (b t) p d", p=P)
    tiles_of = lambda w: w.rearrange("l (k p) n -> p (l k) n", p=P)
    ada_t, in_t, gate_t, wo_t, ff1_t = map(tiles_of, (w_ada, w_in, w_gate, w_o, w_ff1))
    osb_t, ofx_t, ff2_t = map(tiles_of, (w_out_sb, w_out_fox, w_ff2))
    rows_of = lambda v: v.rearrange("l (r q) -> (l r) q", q=P)
    xT_dram = nc.dram_tensor("xT_dram", [KT, P, T], F32, kind="Internal").ap()
    gates_dram = nc.dram_tensor("gates_dram", [2 * KT, P, T], F32, kind="Internal").ap()
    fparts_dram = nc.dram_tensor("fparts_dram", [HEADS, 3, T], BF16, kind="Internal").ap()

    base = (nc.sbuf_base + 31) // 32 * 32
    KB = 1024
    R1, R2, R3, R4, R5, R6 = (base + n * KB for n in (0, 64, 128, 160, 184, 196))
    R7 = base + 204 * KB

    def at(name, offset, shape, dtype):
        return nc.alloc_sbuf_tensor_at(name, shape, dtype, offset=offset)

    ada_first = at("ada_first", R1, [P, 2 * KT, D], F32)
    h1 = [at(f"h1_{s}", R1 + n * 32 * KB, [P, KT, T], F32R) for n, s in enumerate(("hi", "lo"))]
    o_split = [at(f"o_{s}", R1 + n * 32 * KB, [P, KT, T], F32R) for n, s in enumerate(("hi", "lo"))]
    h2 = [at(f"h2_{s}", R1 + n * 32 * KB, [P, KT, T], F32R) for n, s in enumerate(("hi", "lo"))]
    y_nat = at("y_nat", R1, [P, QB, D], F32)
    gain_row = at("gain_row", R1 + 32 * KB, [P, D], F32)
    x_in = at("x_in", R2, [P, KT, T], F32)
    x_scaled = at("x_scaled", R2, [P, KT, T], F32)
    sq_a = at("sq_a", R2 + 32 * KB, [P, 2, D], F32)
    diag_a = at("diag_a", R2 + 40 * KB, [P, QB, P], F32)
    pack1 = at("pack1", R2 + 48 * KB, [PACK1, P], F32)
    pack2 = at("pack2", R2 + 49 * KB, [PACK2, P], F32)
    q_hi = [at(f"q_hi{h}", R2 + 4 * h * KB, [P, T], F32R) for h in range(2)]
    q_lo = [at(f"q_lo{h}", R2 + (8 + 4 * h) * KB, [P, T], F32R) for h in range(2)]
    k_st = [at(f"k_st{h}", R2 + (16 + 4 * h) * KB, [P, T], F32R) for h in range(2)]
    v_st = at("v_st", R2 + 24 * KB, [P, QB, 2, 2, DH], F32R)
    prob = at("prob", R2 + 32 * KB, [P, 2, T], F32)
    surv = at("surv", R2 + 40 * KB, [P, 2, T], F32)
    wT = [at(f"wT_{s}", R2 + (48 + 8 * n) * KB, [P, QB, 2 * P], F32R) for n, s in enumerate(("hi", "lo"))]
    f_abs = at("f_abs", R2 + 40 * KB, [HEADS, T], F32)
    f_log = at("f_log", R2 + 44 * KB, [HEADS, T], F32)
    f_cum = at("f_cum", R2 + 48 * KB, [HEADS, T], F32)
    f_rest = at("f_rest", R2 + 52 * KB, [HEADS, T], F32)
    f_parts = at("f_parts", R2 + 56 * KB, [HEADS, 3, T], BF16)
    merged = [at(f"merged_{s}", R2 + n * 32 * KB, [P, KT, T], F32R) for n, s in enumerate(("hi", "lo"))]
    hid = [at(f"hid_{s}", R2 + n * 32 * KB, [P, KT, T], F32R) for n, s in enumerate(("hi", "lo"))]
    xT = at("xT", R3, [P, KT, T], F32)
    mixed = at("mixed", R3, [P, KT, T], F32)
    res = at("res", R3, [P, KT, T], F32)
    w_raw = [at(f"w_raw{b}", R4 + 4 * b * KB, [P, KT, P], F32) for b in range(2)]
    w_hi = [at(f"w_hi{b}", R4 + (8 + 4 * b) * KB, [P, KT, P], F32R) for b in range(2)]
    w_lo = [at(f"w_lo{b}", R4 + (16 + 4 * b) * KB, [P, KT, P], F32R) for b in range(2)]
    ada = at("ada", R5, [P, 2, D], F32)
    ada_sum = at("ada_sum", R5 + 8 * KB, [P, D], F32)
    q_f = [at(f"q_f{h}", R5 + 4 * h * KB, [6, T], BF16) for h in range(2)]
    k_f = [at(f"k_f{h}", R5 + (4 * h + 2) * KB, [6, T], BF16) for h in range(2)]
    gates = at("gates", R5, [P, 2, 2, T], F32)
    ss_b = at("ss_b", R5, [P, T], F32)
    diag_b = at("diag_b", R5 + 4 * KB, [P, QB, P], F32)
    sq_b = at("sq_b", R5 + 8 * KB, [P, 2, HALF], F32)
    gate_st = at("gate_st", R6, [P, 2, HALF], F32)
    vT = at("vT", R6, [P, T], F32)
    fold = at("fold", R6 + 4 * KB, [P, 2 * P], F32)
    x_again = at("x_again", R6 + 4 * KB, [P, 2, HALF], F32)
    norm_b = at("norm_b", R6, [P, 2, T], F32)
    relu = at("relu", R6, [P, 2, HALF], F32)
    relu_sq = at("relu_sq", R6 + 4 * KB, [P, 2, HALF], F32)
    y_st = at("y_st", R6, [P, 2, T], F32)
    spot = [R7]

    def small(name, shape, dtype):
        n = 1
        for s in shape[1:]:
            n *= s
        t = at(name, spot[0], shape, dtype)
        spot[0] += (n * (2 if dtype == BF16 else 4) + 31) // 32 * 32
        assert spot[0] <= nc.sbuf_usable_end
        return t

    ident = small("ident", [P, P], F32)
    ones = small("ones", [P, P], F32)
    ident_b = small("ident_b", [P, P], BF16)
    mask_b = [small(f"mask_b{m}", [P, P], BF16) for m in range(2)]
    cols = small("cols", [P, PACK1 + PACK2], F32)
    mod = small("mod", [P, N_MOD * KT], F32)
    g_sc = [small(f"g_sc{n}", [P, KT], F32) for n in range(2)]
    gt_b = small("gt_b", [P, KT], F32)
    w_f_raw = small("w_f_raw", [P, KT, HEADS], F32)
    w_f_hi = small("w_f_hi", [P, KT, HEADS], F32R)
    w_f_lo = small("w_f_lo", [P, KT, HEADS], F32R)
    eps_col = small("eps_col", [P, 1], F32)
    rms = [small(f"rms{n}", [P, QB], F32) for n in range(3)]
    rstd = [small(f"rstd{n}", [P, QB], F32) for n in range(3)]
    bf_col = small("bf_col", [HEADS, 1], F32)
    neg_max = small("neg_max", [P, 2], F32)
    row_sum = small("row_sum", [P, 2], F32)
    inv_sum = small("inv_sum", [P, 2], F32)

    with ExitStack() as ctx:
        ps = ctx.enter_context(nc.psum_tensor("ps", [P, 8, HALF], F32))
        scores = [ps[:, 2 * s:2 * s + 2, :].rearrange("p a b -> p (a b)") for s in range(2)]
        sem = lambda name: ctx.enter_context(nc.semaphore(name))

        consts_made = sem("consts_made")
        identity_made = sem("identity_made")
        small_loaded = sem("small_loaded")
        x_loaded = [sem(f"x_loaded{t}") for t in range(QB)]
        x_squared, diag_made, rstd_spread = sem("x_squared"), sem("diag_made"), sem("rstd_spread")
        ada_times_c, ada_part = sem("ada_times_c"), sem("ada_part")
        ada_in = [sem(f"ada_in{j}") for j in range(2 * KT)]
        pack_turned, cols_made = sem("pack_turned"), sem("cols_made")
        ada_loaded = [sem(f"ada_loaded{b}") for b in range(2)]
        ada_used, ada_summed, mod_made, mod_derived = (sem(n) for n in ("ada_used", "ada_summed", "mod_made", "mod_derived"))
        x_turned, x_kept_act, x_kept_dve, x_saved = (sem(n) for n in ("x_turned", "x_kept_act", "x_kept_dve", "x_saved"))
        squared, sq_summed, stats_done, root_done, rstd_made = (
            sem(n) for n in ("squared", "sq_summed", "stats_done", "root_done", "rstd_made"))
        normed, h_hi, h_ready = sem("normed"), sem("h_hi"), sem("h_ready")
        w_loaded = [sem(f"w_loaded{b}") for b in range(2)]
        hi_split = [sem(f"hi_split{b}") for b in range(2)]
        w_split = [sem(f"w_split{b}") for b in range(2)]
        f_w_loaded, f_w_split = sem("f_w_loaded"), sem("f_w_split")
        dense_done, dense_free = sem("dense_done"), sem("dense_free")
        f_step_dve, f_step_act, f_stored, f_loaded, f_ones = (
            sem(n) for n in ("f_step_dve", "f_step_act", "f_stored", "f_loaded", "f_ones"))
        v_copied, k_hi_done, q_hi_done = sem("v_copied"), sem("k_hi_done"), sem("q_hi_done")
        scores_ready, scores_used = sem("scores_ready"), sem("scores_used")
        scanned, max_ready, inv_ready, probs_ready = (sem(n) for n in ("scanned", "max_ready", "inv_ready", "probs_ready"))
        tp_done, tp_hi, tp_free = sem("tp_done"), sem("tp_hi"), sem("tp_free")
        av_done, av_folded, av_free = sem("av_done"), sem("av_folded"), sem("av_free")
        gate_done, gate_copied = sem("gate_done"), sem("gate_copied")
        gate_saved = [sem(f"gate_saved{b}") for b in range(2)]
        gate_back = [sem(f"gate_back{b}") for b in range(2)]
        o_hi_done, o_ready = sem("o_hi_done"), sem("o_ready")
        gate_on, merge_mul, merge_sum, merge_hi = (sem(n) for n in ("gate_on", "merge_mul", "merge_sum", "merge_hi"))
        x_back = [sem(f"x_back{b}") for b in range(2)]
        act_free, hid_hi, relu_squared, hid_ready = (sem(n) for n in ("act_free", "hid_hi", "relu_squared", "hid_ready"))
        gain_loaded, y_turned, y_kept, out_saved = (sem(n) for n in ("gain_loaded", "y_turned", "y_kept", "out_saved"))
        y_scaled = [sem(f"y_scaled{b}") for b in range(2)]

        block = ctx.enter_context(nc.Block())

        @block.sync
        def _(sp):
            for t in range(KT):
                sp.dma_start(x_in[:, t, :], x_rows[t]).then_inc(x_loaded[t], 16)
            for r, v in ((COL_GMIX, g_mix), (COL_GMLP, g_mlp), (COL_BGATE, b_gate), (COL_BFF1, b_ff1),
                         (COL_C, c), (COL_BFF2, b_ff2)):
                src = rows_of(v)
                sp.dma_start(pack1[r:r + src.shape[0], :], src).then_inc(small_loaded, 16)
            sp.dma_start(pack2[:, :], rows_of(b_ada)).then_inc(small_loaded, 16)
            sp.dma_start(bf_col[:, :], b_f.rearrange("l h -> h l")).then_inc(small_loaded, 16)
            sp.dma_start(w_f_raw[:, :, :], in_t[:, :, 6 * D_MIX:6 * D_MIX + HEADS]).then_inc(f_w_loaded, 16)
            for j in range(2 * KT):
                m, k = 1 - j // KT, j % KT
                sp.dma_start(ada_first[:, j, :], ada_t[:, k, D * m:D * m + D]).then_inc(ada_in[j], 16)

            def load_ada(m, k):
                sp.wait_ge(ada_used, ADA_FIRST + KT * (m - 2) + k - 1)
                sp.dma_start(ada[:, k % 2, :], ada_t[:, k, bass.ds(D * m, D)]).then_inc(ada_loaded[k % 2], 16)

            def load_w(b, use, parts):
                sp.wait_ge(w_split[b], START + 2 * use)
                for hf in (1, 0):
                    sp.dma_start(w_raw[b][:, 4 * hf:4 * hf + 4, :], parts[hf]).then_inc(w_loaded[b], 16)

            halves = lambda w, col: [w[:, 0:4, bass.ds(col, P)], w[:, 4:8, bass.ds(col, P)]]

            def pair_loads(G, k_col, q_col, v_col, fox):
                load_w(0, 2 * G, halves(in_t, q_col))
                load_w(1, 3 * G, halves(in_t, k_col))
                if not fox:
                    load_ada(G + 2, 0)
                    load_ada(G + 2, 1)
                load_w(0, 2 * G + 1, halves(in_t, v_col))
                if not fox:
                    load_ada(G + 2, 2)
                    load_ada(G + 2, 3)
                    load_ada(G + 2, 4)
                    load_ada(G + 2, 5)
                else:
                    sp.wait_ge(f_stored, 16)
                    sp.wait_ge(f_ones, 4)
                    sp.wait_ge(scores_ready, UNITS * G)
                    for h in range(2):
                        src = fparts_dram[bass.ds(2 * (G - PAIRS) + h, 1)].rearrange("a r t -> (a r) t")
                        sp.dma_start(q_f[h][0:3, :], src).then_inc(f_loaded, 16)
                        sp.dma_start(k_f[h][3:6, :], src).then_inc(f_loaded, 16)
                load_w(1, 3 * G + 1, halves(gate_t, 2 * P * G))
                if not fox:
                    load_ada(G + 2, 6)
                    load_ada(G + 2, 7)
                load_w(1, 3 * G + 2, halves(gate_t, 2 * P * G + P))

            with sp.Fori(0, PAIRS) as G:
                pair_loads(G, D_MIX + P * G, P * G, 2 * D_MIX + P * G, False)
            with sp.Fori(PAIRS, 2 * PAIRS) as G:
                at_g = 3 * D_MIX - P * PAIRS + P * G
                pair_loads(G, at_g + D_MIX, at_g, at_g + 2 * D_MIX, True)
            for n in range(KT):
                load_w(n % 2, USE_MERGE[n % 2] + n // 2, [osb_t[:, :, P * n:P * n + P], ofx_t[:, :, P * n:P * n + P]])
            with sp.Fori(0, KT // 2) as n:
                for b in range(2):
                    load_w(b, USE_WO[b] + n, halves(wo_t, 2 * P * n + P * b))
            with sp.Fori(0, FF_CHUNKS) as ch:
                with sp.Fori(0, KT // 2) as n:
                    for b in range(2):
                        load_w(b, USE_FF[b] + KT * ch + n, halves(ff1_t, D * ch + 2 * P * n + P * b))
                with sp.Fori(0, KT // 2) as n:
                    for b in range(2):
                        col = 2 * P * n + P * b
                        load_w(b, USE_FF[b] + KT * ch + KT // 2 + n,
                               [ff2_t[:, bass.ds(KT * ch + 4 * hf, 4), bass.ds(col, P)] for hf in range(2)])
            scaled_by = [0, 0]
            for t in OUT_ORDER:
                by = int(t in SCALED_BY_ACT[0] + SCALED_BY_ACT[1])
                scaled_by[by] += 1
                sp.wait_ge(y_scaled[by], scaled_by[by])
                sp.dma_start(out_rows[t], y_nat[:, t, :]).then_inc(out_saved, 16)
            sp.wait_ge(out_saved, 16 * QB)

        @block.gpsimd
        def _(pool):
            for b in range(2):
                pool.sem_inc(w_split[b], START)
            nc.gpsimd.memset(ident[:, :], 0.0).then_inc(identity_made, 1)
            nc.gpsimd.memset(ident_b[:, :], 0.0).then_inc(identity_made, 1)
            for m in range(2):
                nc.gpsimd.memset(mask_b[m][:, :], 0.0).then_inc(identity_made, 1)
            nc.gpsimd.memset(ones[:, :], 1.0).then_inc(consts_made, 1)
            nc.gpsimd.memset(eps_col[:, :], EPS).then_inc(consts_made, 1)
            pool.wait_ge(identity_made, 4)
            for t in (ident, ident_b):
                nc.gpsimd.affine_select(out=t[:, :], in_=t[:, :], compare_op=ALU.not_equal, fill=1.0, base=0,
                                        pattern=[[-1, P]], channel_multiplier=1).then_inc(consts_made, 1)
            for m, op in enumerate((ALU.is_gt, ALU.is_ge)):
                nc.gpsimd.affine_select(out=mask_b[m][:, :], in_=mask_b[m][:, :], compare_op=op, fill=NEG, base=0,
                                        pattern=[[-1, P]], channel_multiplier=1).then_inc(consts_made, 1)

            def split(b, use):
                one = ones[:, :].unsqueeze(1).broadcast_to([P, 4, P])
                pool.wait_ge(w_loaded[b], 32 * use + 32)
                for hf in range(2):
                    raw = w_raw[b][:, 4 * hf:4 * hf + 4, :]
                    hi = w_hi[b][:, 4 * hf:4 * hf + 4, :]
                    lo = w_lo[b][:, 4 * hf:4 * hf + 4, :]
                    nc.gpsimd.tensor_tensor(hi, raw, one, ALU.mult).then_inc(hi_split[b], 1)
                    pool.wait_ge(hi_split[b], 2 * use + hf + 1)
                    nc.gpsimd.tensor_tensor(lo, raw, hi.bitcast(F32), ALU.subtract).then_inc(w_split[b], 1)

            pool.wait_ge(f_w_loaded, 16)
            pool.wait_ge(consts_made, 2)
            nc.gpsimd.tensor_tensor(w_f_hi[:, :, :], w_f_raw[:, :, :], ones[:, 0:HEADS].unsqueeze(1).broadcast_to([P, KT, HEADS]),
                                    ALU.mult).then_inc(f_w_split, 1)
            pool.wait_ge(f_w_split, 1)
            nc.gpsimd.tensor_tensor(w_f_lo[:, :, :], w_f_raw[:, :, :], w_f_hi[:, :, :].bitcast(F32),
                                    ALU.subtract).then_inc(f_w_split, 1)
            for k in range(1, KT // 2):
                pool.wait_ge(ada_times_c, k + 1)
                if k > 1:
                    pool.wait_ge(ada_part, k - 1)
                nc.gpsimd.tensor_tensor(ada_first[:, KT, :], ada_first[:, KT, :], ada_first[:, KT + k, :],
                                        ALU.add).then_inc(ada_part, 1)
            split(0, 0)
            split(1, 0)
            with pool.Fori(0, 2 * PAIRS) as G:
                done = DONE_F + DONE_ITER * G
                pool.wait_ge(dense_done, done + 2)
                split(0, 2 * G + 1)
                pool.wait_ge(dense_done, done + 4)
                split(1, 3 * G + 1)
                pool.wait_ge(dense_done, done + 6)
                split(0, 2 * G + 2)
                pool.wait_ge(gate_done, START + 4 * G + 2)
                split(1, 3 * G + 2)
                pool.wait_ge(gate_done, START + 4 * G + 4)
                split(1, 3 * G + 3)
            with pool.Fori(1, KT // 2) as n:
                for b in range(2):
                    pool.wait_ge(dense_done, DONE_MERGE - 4 + 4 * (2 * n + b))
                    split(b, USE_MERGE[b] + n)
            with pool.Fori(0, KT // 2) as n:
                for b in range(2):
                    pool.wait_ge(dense_done, DONE_WO - 2 + 2 * (2 * n + b))
                    split(b, USE_WO[b] + n)
            with pool.Fori(0, FF_CHUNKS * KT) as n:
                for b in range(2):
                    pool.wait_ge(dense_done, DONE_FF - 2 + 2 * (2 * n + b))
                    split(b, USE_FF[b] + n)

        @block.tensor
        def _(pe):
            pe.sem_inc(gate_done, START)
            pe.sem_inc(av_done, START)

            def three(dst, b, k, rhs, cols_, start, stop, w=None):
                hi, lo = w or (w_hi[b], w_lo[b])
                pe.matmul(dst, hi[:, k, :], rhs[0][:, k, cols_], start=start, stop=False)
                pe.matmul(dst, hi[:, k, :], rhs[1][:, k, cols_], start=False, stop=False)
                return pe.matmul(dst, lo[:, k, :], rhs[0][:, k, cols_], start=False, stop=stop)

            halves = [slice(0, HALF), slice(HALF, T)]

            def dense(b, use, rhs, bank, ready=None, midway=None):
                for k in range(KT):
                    if k == KT // 2 and midway is not None:
                        midway()
                    if k % 4 == 0:
                        pe.wait_ge(w_split[b], START + 2 * use + k // 4 + 1)
                    if ready is not None:
                        pe.wait_ge(*ready(k))
                    for hf in range(2):
                        mm = three(ps[:, bank + hf, :], b, k, rhs, halves[hf], k == 0, k == KT - 1)
                        if k == KT - 1:
                            mm.then_inc(dense_done, 1)

            def ada_total(steps):
                pe.wait_ge(ada_used, steps)
                for n in range(KT):
                    mm = pe.matmul(ps[:, 6, n:n + 1], ada_sum[:, P * n:P * n + P], ones[:, 0:1], start=True, stop=True)
                mm.then_inc(ada_summed, 1)

            def token_sums(hf):
                for t in range(4 * hf, 4 * hf + 4):
                    mm = pe.matmul(ps[:, 0, t:t + 1], ss_b[:, P * t:P * t + P], ones[:, 0:1], start=True, stop=True)
                mm.then_inc(stats_done, 1)

            def spread_rstd(which, tiles):
                diag = (diag_a, diag_b)[which]
                for t in tiles:
                    pe.wait_ge(diag_made, QB * which + t + 1)
                    mm = pe.matmul(ps[:, 4 + t // 4, P * (t % 4):P * (t % 4) + P], ones[:, :], diag[:, t, :],
                                   start=True, stop=True)
                if t == QB - 1:
                    mm.then_inc(rstd_spread, 1)

            def dense_by_half(b, use, rhs, bank, ready, between):
                for hf in range(2):
                    for k in range(KT):
                        if (hf, k) in between:
                            between[hf, k]()
                        if hf == 0 and k % 4 == 0:
                            pe.wait_ge(w_split[b], START + 2 * use + k // 4 + 1)
                        if hf == 0:
                            pe.wait_ge(*ready(k))
                        mm = three(ps[:, bank + hf, :], b, k, rhs, halves[hf], k == 0, k == KT - 1)
                    mm.then_inc(dense_done, 1)

            pe.wait_ge(consts_made, 6)
            for t in range(QB):
                pe.wait_ge(x_loaded[t], 16)
                if t >= 2:
                    pe.wait_ge(x_kept_act, t - 1)
                    pe.wait_ge(x_kept_dve, t - 1)
                for k in range(KT):
                    mm = pe.transpose(ps[:, 2 * (t % 2) + k // 4, P * (k % 4):P * (k % 4) + P],
                                      x_in[:, t, P * k:P * k + P], ident[:, :])
                    if k % 4 == 3:
                        mm.then_inc(x_turned, 1)
            pe.wait_ge(small_loaded, 16 * 8)
            pe.transpose(ps[:, 6, 0:PACK1], pack1[:, :], ident[0:PACK1, 0:PACK1])
            pe.transpose(ps[:, 6, PACK1:PACK1 + PACK2], pack2[:, :], ident[0:PACK2, 0:PACK2]).then_inc(pack_turned, 1)
            spread_rstd(0, range(QB))
            pe.wait_ge(cols_made, 1)
            ada_total(KT)
            pe.wait_ge(mod_made, 1)
            ada_total(ADA_FIRST)
            pe.wait_ge(f_w_split, 2)
            for k in range(KT):
                pe.wait_ge(h_ready, k + 1)
                for hf in range(2):
                    mm = three(ps[0:HEADS, 2 + hf, :], None, k, h1, halves[hf], k == 0, k == KT - 1, (w_f_hi, w_f_lo))
                    if k == KT - 1:
                        mm.then_inc(dense_done, 1)

            def queries(G):
                pe.wait_ge(scores_used, START + UNITS * G)
                dense(0, 2 * G, h1, 0)

            def attend(G, fox, final=False):
                pe.wait_ge(dense_free, FREE_F + FREE_ITER * G)
                dense(1, 3 * G, h1, 2)
                pe.wait_ge(av_free, START + QB * G)
                pe.wait_ge(gate_copied, START + 4 * G)
                pe.wait_ge(mod_made, 2)
                dense(0, 2 * G + 1, h1, 6)

                def turn(idx, blocks, src):
                    if idx == 0:
                        pe.wait_ge(tp_free, START + TP_ITER * G)
                    else:
                        pe.wait_ge(tp_free, START + TP_ITER * G + idx - 1)
                    for n, blk in enumerate(blocks):
                        mm = pe.transpose(ps[:, 4 + idx % 2, P * n:P * n + P], src[:, P * blk:P * blk + P], ident[:, :])
                    mm.then_inc(tp_done, 1)

                def turn_values():
                    pe.wait_ge(v_copied, 2 * G + 2)
                    for idx in range(V_CHUNKS):
                        turn(idx, range(4 * idx, 4 * idx + 4), vT)

                def score(u):
                    h, i = divmod(u, QB)
                    if u < 2:
                        pe.wait_ge(dense_free, FREE_F + FREE_ITER * (G + 1))
                        if fox and u == 0:
                            pe.wait_ge(f_loaded, 64 * (G - PAIRS + 1))
                    else:
                        pe.wait_ge(scores_used, START + UNITS * G + u - 1)
                    n = P * (i + 1)
                    qs = slice(P * i, P * i + P)
                    for c0 in range(0, n, HALF):
                        ks = slice(c0, min(c0 + HALF, n))
                        dst = scores[u % 2][:, ks]
                        pe.matmul(dst, q_hi[h][:, qs], k_st[h][:, ks], start=True, stop=False)
                        if fox:
                            pe.matmul(dst, q_f[h][:, qs], k_f[h][:, ks], start=False, stop=False)
                        if c0 + HALF >= n:
                            pe.matmul(scores[u % 2][:, n - P:n], ident_b[:, :], mask_b[int(fox)][:, :],
                                      start=False, stop=False)
                        mm = pe.matmul(dst, q_lo[h][:, qs], k_st[h][:, ks], start=False, stop=True)
                    mm.then_inc(scores_ready, 1)

                def turn_probs(u):
                    pe.wait_ge(probs_ready, UNITS * G + u + 1)
                    i = u % QB
                    for n, idx in enumerate(chunks_of(u)):
                        turn(idx, range(4 * n, min(4 * n + 4, i + 1)), prob[:, u % 2, :])

                def values(u):
                    h, i = divmod(u, QB)
                    pe.wait_ge(tp_free, START + TP_ITER * G + chunks_of(u)[-1] + 1)
                    pe.wait_ge(av_free, START + QB * G + u // 2)
                    if u == 1 and not fox:
                        pe.wait_ge(mod_made, G + 3)
                    for kb in range(i + 1):
                        q0 = P if kb == i else 0
                        for s in range(2):
                            mm = pe.matmul(ps[:, 6, q0:2 * P], v_st[:, kb, h, :, :].rearrange("p a d -> p (a d)"),
                                           wT[s][:, kb, q0:2 * P], start=(kb == 0 and s == 0), stop=(kb == i and s == 1))
                    mm.then_inc(av_done, 1)

                def gate_step(n):
                    tile, hf, quarter = n // 8, n // 4 % 2, n % 4
                    if n == 0:
                        pe.wait_ge(v_copied, 2 * G + 2)
                    elif quarter == 0:
                        pe.wait_ge(gate_copied, START + 4 * G + n // 4)
                    if quarter % 2 == 0:
                        pe.wait_ge(w_split[1], START + 2 * (3 * G + 1 + tile) + quarter // 2 + 1)
                    for k in (2 * quarter, 2 * quarter + 1):
                        mm = three(ps[:, 7, :], 1, k, h1, halves[hf], k == 0, k == KT - 1)
                    if k == KT - 1:
                        mm.then_inc(gate_done, 1)

                def gates_at(s):
                    for n, at_step in enumerate(GATE_STEPS):
                        if at_step == s:
                            gate_step(n)

                for s in range(STEPS):
                    if s == STEPS - 1 and not final:
                        queries(G + 1)
                    if s < UNITS:
                        score(s)
                    if s == 1:
                        turn_values()
                    if s == 2 and not fox:
                        ada_total(ADA_FIRST + KT * (G + 1))
                    if s in GATES_FIRST:
                        gates_at(s)
                    if s >= 3 and s % 2 == 0:
                        values(s - 3)
                    if 2 <= s < UNITS + 2:
                        turn_probs(s - 2)
                    if s not in GATES_FIRST:
                        gates_at(s)

            queries(0)
            with pe.Fori(0, PAIRS) as G:
                attend(G, False)
            with pe.Fori(PAIRS, 2 * PAIRS - 1) as G:
                attend(G, True)
            attend(2 * PAIRS - 1, True, final=True)

            pe.wait_ge(scores_used, START + 2 * PAIRS * UNITS)
            with pe.Fori(0, KT // 2) as n:
                for b in range(2):
                    if b == 1:
                        pe.wait_ge(tp_free, START + 2 * PAIRS * TP_ITER)
                        pe.wait_ge(av_free, START + 2 * PAIRS * QB)
                        pe.wait_ge(gate_copied, START + 8 * PAIRS)
                    pe.wait_ge(dense_free, FREE_MERGE - 2 + 2 * (2 * n + b))
                    for k in range(KT):
                        if k % 4 == 0:
                            pe.wait_ge(w_split[b], START + 2 * (USE_MERGE[b] + n) + k // 4 + 1)
                        pe.wait_ge(o_ready, k + 1)
                        for hf in range(2):
                            mm = three(ps[:, 4 * b + 2 * (k // 4) + hf, :], b, k, o_split, halves[hf],
                                       k % 4 == 0, k % 4 == 3)
                            if k % 4 == 3:
                                mm.then_inc(dense_done, 1)
            merged_ready = lambda k: (dense_free, FREE_MERGE + 2 * k + 2)

            def wo_tile(n, b):
                pe.wait_ge(dense_free, FREE_WO - 2 + 2 * (2 * n + b))
                dense(b, USE_WO[b] + n, merged, 2 * b, ready=merged_ready)

            with pe.Fori(0, KT // 2 - 1) as n:
                for b in range(2):
                    wo_tile(n, b)
            wo_tile(KT // 2 - 1, 0)
            pe.wait_ge(dense_free, FREE_WO - 2 + 2 * (KT - 1))

            def first_sums():
                pe.wait_ge(sq_summed, 2 * KT - 1)
                token_sums(0)

            dense_by_half(1, USE_WO[1] + KT // 2 - 1, merged, 2, merged_ready, {(1, KT // 2): first_sums})
            spread_rstd(1, range(QB // 2))
            pe.wait_ge(sq_summed, 2 * KT)
            token_sums(1)
            spread_rstd(1, range(QB // 2, QB))
            for b in range(2):
                pe.wait_ge(dense_free, FREE_FF)
            for at_k in range(KT + 2):
                for b in range(2):
                    k = at_k - 2 * b
                    if not 0 <= k < KT:
                        continue
                    if k % 4 == 0:
                        pe.wait_ge(w_split[b], START + 2 * USE_FF[b] + k // 4 + 1)
                    pe.wait_ge(h_ready, KT + k + 1)
                    for hf in range(2):
                        mm = three(ps[:, 2 * b + hf, :], b, k, h2, halves[hf], k == 0, k == KT - 1)
                        if k == KT - 1:
                            mm.then_inc(dense_done, 1)

            def ff1_pair(ch, n):
                for b in range(2):
                    pe.wait_ge(dense_free, FREE_FF - 2 + 2 * KT * ch + 2 * b)
                    pe.wait_ge(act_free, KT - 2 + 2 * KT * ch + 2 * (2 * n + b))
                    dense(b, USE_FF[b] + KT * ch + n, h2, 2 * b)

            def ff2_tile(ch, n, b, midway=None):
                pe.wait_ge(dense_free, FREE_FF - 2 + 2 * KT * ch + 2 * (2 * n + b))
                pe.wait_ge(act_free, KT + 2 * KT * ch + 14 + 2 * b)
                dense(b, USE_FF[b] + KT * ch + KT // 2 + n, hid, 2 * b,
                      ready=lambda k: (hid_ready, START + 2 * KT * ch + 2 * k + 2), midway=midway)

            with pe.Fori(1, KT // 2) as n:
                ff1_pair(0, n)
            with pe.Fori(0, KT // 2) as n:
                for b in range(2):
                    ff2_tile(0, n, b)
            with pe.Fori(1, FF_CHUNKS - 1) as ch:
                with pe.Fori(0, KT // 2) as n:
                    ff1_pair(ch, n)
                with pe.Fori(0, KT // 2) as n:
                    for b in range(2):
                        ff2_tile(ch, n, b)
            LAST = FF_CHUNKS - 1
            with pe.Fori(0, KT // 2) as n:
                ff1_pair(LAST, n)

            def turn_back(tile, b, hfs=(0, 1)):
                pe.wait_ge(y_kept, START + 2 * tile - 2 * b)
                for hf in hfs:
                    pe.wait_ge(dense_free, FREE_LAST + 2 * tile + hf + 1)
                    for t in range(4 * hf, 4 * hf + 4):
                        mm = pe.transpose(ps[:, 4 + 2 * b + hf, P * (t % 4):P * (t % 4) + P],
                                          y_st[:, b, P * t:P * t + P], ident[:, :])
                    mm.then_inc(y_turned, 1)

            def last_pair(n, first):
                ff2_tile(LAST, n, 0, None if first else lambda: turn_back(2 * n - 1, 1))
                ff2_tile(LAST, n, 1, lambda: turn_back(2 * n, 0))

            last_pair(0, True)
            with pe.Fori(1, KT // 2 - 1) as n:
                last_pair(n, False)
            n = KT // 2 - 1
            ff2_tile(LAST, n, 0, lambda: turn_back(2 * n - 1, 1))

            def first_half():
                turn_back(KT - 1, 1, hfs=(0,))
                pe.wait_ge(sq_summed, 4 * KT - 1)
                token_sums(0)

            pe.wait_ge(dense_free, FREE_LAST - 2 + 2 * (KT - 1))
            dense_by_half(1, USE_FF[1] + KT * LAST + KT // 2 + n, hid, 2,
                          lambda k: (hid_ready, START + 2 * KT * LAST + 2 * k + 2),
                          {(0, KT // 2): lambda: turn_back(KT - 2, 0), (1, KT // 2): first_half})
            turn_back(KT - 1, 1, hfs=(1,))
            pe.wait_ge(root_done, 4)
            pe.wait_ge(sq_summed, 4 * KT)
            token_sums(1)

        @block.scalar
        def _(act):
            act.sem_inc(scores_used, START)
            act.sem_inc(gate_copied, START)
            for b in range(2):
                act.sem_inc(gate_saved[b], 16 * START)
            A = nc.scalar.activation
            halves = [slice(0, HALF), slice(HALF, T)]
            carrier = act.alloc_register("wait_carrier")
            carried = [0]

            def carry():
                carried[0] ^= 1
                act.reg_mov(carrier, carried[0])

            def norm_hi(which, k, tmp, h):
                act.wait_ge(normed, KT * which + k + 1)
                A(h[0][:, k, :], tmp, ACT.Identity,
                  bias=mod[:, 3 * KT * which + k:3 * KT * which + k + 1]).then_inc(h_hi, 1)

            act.wait_ge(consts_made, 6)
            for t in range(QB):
                act.wait_ge(x_loaded[t], 16)
                if t >= 2:
                    act.wait_ge(x_squared, t - 1)
                A(sq_a[:, t % 2, :], x_in[:, t, :], ACT.Square, accum_out=rms[0][:, t:t + 1]).then_inc(x_squared, 1)
                act.wait_ge(x_turned, 2 * t + 1)
                A(xT[:, 0:KT // 2, P * t:P * t + P], ps[:, 2 * (t % 2), :].rearrange("p (k t) -> p k t", t=P),
                  ACT.Copy).then_inc(x_kept_act, 1)
            act.wait_ge(x_squared, QB)
            A(rms[0][:, :], rms[0][:, :], ACT.Sqrt, bias=eps_col[:, 0:1], scale=1.0 / D).then_inc(root_done, 1)
            act.wait_ge(cols_made, 1)
            for k in range(KT // 2):
                act.wait_ge(ada_in[KT + k], 16)
                A(ada_first[:, KT + k, :], ada_first[:, KT + k, :], ACT.Copy, scale=cols[:, COL_C + k:COL_C + k + 1]
                  ).then_inc(ada_times_c, 1)
            act.wait_ge(x_kept_act, QB)
            act.wait_ge(x_kept_dve, QB)
            act.dma_start(xT_dram.rearrange("k p t -> p k t"), xT[:, :, :]).then_inc(x_saved, 16)
            act.wait_ge(mod_made, 2)
            for k in range(KT):
                norm_hi(0, k, x_scaled[:, k, :], h1)
            act.wait_ge(dense_done, DONE_F)
            A(f_abs[:, :], ps[0:HEADS, 2:4, :].rearrange("p a b -> p (a b)"), ACT.Abs,
              bias=bf_col[:, 0:1]).then_inc(f_step_act, 1)
            act.wait_ge(f_step_act, 1)
            A(f_abs[:, :], f_abs[:, :], ACT.Exp, scale=-1.0).then_inc(f_step_act, 1)
            act.wait_ge(f_step_act, 2)
            A(f_abs[:, :], f_abs[:, :], ACT.Ln, bias=ones[0:HEADS, 0:1]).then_inc(f_step_act, 1)
            act.wait_ge(f_step_dve, 7)
            act.dma_start(fparts_dram, f_parts[:, :, :]).then_inc(f_stored, 16)

            def outputs_hi(k):
                act.wait_ge(av_free, START + QB * (k + 1))
                A(o_split[0][:, k, :], mixed[:, k, :], ACT.Copy).then_inc(o_hi_done, 1)

            def attend(G, fox, final=False):
                done = DONE_F + DONE_ITER * G
                for hf in range(2):
                    act.wait_ge(dense_done, done + hf + 1)
                    for h in range(2):
                        rows = slice(DH * h, DH * h + DH)
                        for to in range(2):
                            last = A(q_hi[h][DH * to:DH * to + DH, halves[hf]], ps[rows, hf, :], ACT.Copy, scale=SCALE)
                    last.then_inc(q_hi_done, 1)
                for hf in range(2):
                    act.wait_ge(dense_done, done + 2 + hf + 1)
                    A(k_st[0][0:DH, halves[hf]], ps[0:DH, 2 + hf, :], ACT.Copy)
                    A(k_st[1][DH:P, halves[hf]], ps[DH:P, 2 + hf, :], ACT.Copy).then_inc(k_hi_done, 1)
                for hf in range(2):
                    act.wait_ge(dense_done, done + 4 + hf + 1)
                    act.wait_ge(gate_saved[hf], 16 * START + 32 * G)
                    A(vT[:, halves[hf]], ps[:, 6 + hf, :], ACT.Copy).then_inc(v_copied, 1)

                def values_hi():
                    for idx in range(V_CHUNKS):
                        act.wait_ge(tp_done, TP_ITER * G + idx + 1)
                        A(v_st[:, 4 * idx:4 * idx + 4, :, 0, :],
                          ps[:, 4 + idx, :].rearrange("p (b h d) -> p b h d", h=2, d=DH), ACT.Copy).then_inc(tp_hi, 1)

                def gate_out(q):
                    act.wait_ge(gate_done, START + 4 * G + q + 1)
                    act.wait_ge(gate_saved[q % 2], 16 * START + 16 * (2 * G + q // 2))
                    A(gate_st[:, q % 2, :], ps[:, 7, :], ACT.Copy).then_inc(gate_copied, 1)

                def gate_store(q):
                    act.wait_ge(gate_copied, START + 4 * G + q + 1)
                    act.dma_start(gates_dram[bass.ds(2 * G + q // 2, 1), :, halves[q % 2]].rearrange("a p t -> (a p) t"),
                                  gate_st[:, q % 2, :]).then_inc(gate_saved[q % 2], 16)

                def fold_values(u):
                    h = u // QB
                    own, other = slice(DH * h, DH * h + DH), slice(DH * (1 - h), DH * (1 - h) + DH)
                    act.wait_ge(av_done, START + QB * G + u // 2 + 1)
                    act.wait_ge(av_free, START + QB * G + u // 2)
                    A(fold[own, :], ps[other, 6, 0:2 * P], ACT.Copy).then_inc(av_folded, 1)

                def weights_hi(u):
                    i = u % QB
                    if i % 2 == 0:
                        act.wait_ge(av_done, START + QB * G + u // 2)
                    q0 = P * (i % 2)
                    for n, idx in enumerate(chunks_of(u)):
                        nb = min(4, i + 1 - 4 * n)
                        act.wait_ge(tp_done, TP_ITER * G + idx + 1)
                        A(wT[0][:, 4 * n:4 * n + nb, q0:q0 + P],
                          ps[:, 4 + idx % 2, 0:P * nb].rearrange("p (b q) -> p b q", q=P), ACT.Copy).then_inc(tp_hi, 1)

                def scores_out(u):
                    n = P * (u % QB + 1)
                    act.wait_ge(scores_ready, UNITS * G + u + 1)
                    if u >= 2:
                        act.wait_ge(tp_done, TP_ITER * G + chunks_of(u - 2)[-1] + 1)
                    z = scores[u % 2][:, 0:n]
                    if fox:
                        act.wait_ge(max_ready, UNITS * (G - PAIRS) + u + 1)
                        A(prob[:, u % 2, 0:n], z, ACT.Exp, bias=neg_max[:, u % 2:u % 2 + 1],
                          accum_out=row_sum[:, u % 2:u % 2 + 1]).then_inc(scores_used, 1)
                    else:
                        A(prob[:, u % 2, 0:n], z, ACT.Sigmoid)
                        A(surv[:, u % 2, 0:n], z, ACT.Sigmoid, scale=-1.0).then_inc(scores_used, 1)

                for s in range(STEPS):
                    if s == STEPS - 1 and final:
                        act.wait_ge(gate_done, START + 8 * PAIRS)
                        outputs_hi(0)
                        outputs_hi(1)
                    for q in range(4):
                        if s == GATE_STEPS[4 * q + 3] + 2:
                            gate_store(q)
                        if s == GATE_STEPS[4 * q + 3] + 1:
                            gate_out(q)
                    if s == 1:
                        values_hi()
                    if s >= 3 and s % 2 == 0:
                        fold_values(s - 3)
                    if 2 <= s < UNITS + 2:
                        weights_hi(s - 2)
                    if s < UNITS:
                        scores_out(s)
                gate_store(3)

            with act.Fori(0, PAIRS) as G:
                attend(G, False)
            with act.Fori(PAIRS, 2 * PAIRS - 1) as G:
                attend(G, True)
            attend(2 * PAIRS - 1, True, final=True)

            for k in range(2, KT):
                outputs_hi(k)
            for b in range(2):
                act.wait_ge(gate_saved[b], 16 * START + 16 * 4 * 2 * PAIRS // 2)

            both_mixers = gates_dram.rearrange("(m k) p t -> k p m t", m=2)

            def gates_back(tile, b):
                act.dma_start(gates[:, b, :, :], both_mixers[bass.ds(tile, 1)].rearrange("a p m t -> (a p) m t")
                              ).then_inc(gate_back[b], 16)

            def merge_pair(n, last):
                for b in range(2):
                    act.wait_ge(gate_back[b], 16 * n + 16)
                    carry()
                    for m in range(2):
                        A(gates[:, b, m, :], gates[:, b, m, :], ACT.Sigmoid,
                          bias=cols[:, bass.ds(COL_BGATE + KT * m + 2 * n + b, 1)]).then_inc(gate_on, 1)
                    if not (last and b == 1):
                        act.wait_ge(dense_free, FREE_MERGE + 2 * (2 * n + b))
                        if b == 0:
                            gates_back(2 * n + 1, 1)
                        else:
                            gates_back(2 * n + 2, 0)
                    for hf in range(2):
                        act.wait_ge(merge_sum, 4 * n + 2 * b + hf + 1)
                        carry()
                        A(merged[0][:, bass.ds(2 * n + b, 1), halves[hf]].rearrange("p a t -> p (a t)"),
                          gates[:, b, 0, halves[hf]], ACT.Copy).then_inc(merge_hi, 1)

            act.wait_ge(dense_free, FREE_MERGE)
            gates_back(0, 0)
            with act.Fori(0, KT // 2 - 1) as n:
                merge_pair(n, False)
            merge_pair(KT // 2 - 1, True)
            def root(which, hf):
                act.wait_ge(stats_done, 2 * which - 1 + hf)
                A(rms[which][:, 4 * hf:4 * hf + 4], ps[:, 0, 4 * hf:4 * hf + 4], ACT.Sqrt, bias=eps_col[:, 0:1],
                  scale=1.0 / D).then_inc(root_done, 1)

            def square(n):
                if n >= 2:
                    act.wait_ge(sq_summed, n - 1)
                A(sq_b[:, n % 2, :], res[:, n // 2, halves[n % 2]], ACT.Square).then_inc(squared, 1)

            act.wait_ge(x_saved, 16)
            for k in range(KT):
                for hf in range(2):
                    act.wait_ge(dense_free, FREE_WO - 1 + 2 * k + hf if k else FREE_WO)
                    act.dma_start(x_again[:, hf, :], xT_dram[k, :, halves[hf]]).then_inc(x_back[hf], 16)
                if k:
                    for hf in range(2):
                        square(2 * (k - 1) + hf)
            for hf in range(2):
                act.wait_ge(dense_free, FREE_WO + 2 * (KT - 1) + hf + 1)
                square(2 * (KT - 1) + hf)
                root(1, hf)
            for k in range(KT):
                norm_hi(1, k, norm_b[:, k % 2, :], h2)
                A(res[:, k, :], res[:, k, :], ACT.Identity, bias=gt_b[:, k:k + 1]).then_inc(act_free, 1)
            with act.Fori(0, FF_CHUNKS) as ch:
                with act.Fori(0, KT) as n:
                    for hf in range(2):
                        act.wait_ge(dense_done, DONE_FF + 4 * KT * ch + 2 * n + hf + 1)
                        act.wait_ge(hid_ready, START + 2 * KT * ch + 2 * n + hf)
                        carry()
                        A(relu[:, hf, :], ps[:, bass.ds(2 * (n % 2) + hf, 1), :].rearrange("p a t -> p (a t)"), ACT.Relu,
                          bias=cols[:, bass.ds(COL_BFF1 + KT * ch + n, 1)]).then_inc(act_free, 1)
                        act.wait_ge(act_free, KT + 2 * KT * ch + 2 * n + hf + 1)
                        carry()
                        A(hid[0][:, bass.ds(n, 1), halves[hf]].rearrange("p a t -> p (a t)"), relu[:, hf, :],
                          ACT.Square).then_inc(hid_hi, 1)
            act.wait_ge(dense_done, DONE_FF + 4 * KT * (FF_CHUNKS - 1) + 2 * KT)
            act.dma_start(gain_row[:, :], g_final.rearrange("(l d) -> l d", l=1).partition_broadcast(P)
                          ).then_inc(gain_loaded, 16)

            def last_square(n, b, hf):
                act.wait_ge(dense_free, FREE_LAST + 4 * n + 2 * b + hf + 1)
                act.wait_ge(sq_summed, 2 * KT + 4 * n + 2 * b + hf - 1)
                A(sq_b[:, hf, :], y_st[:, b, halves[hf]], ACT.Square).then_inc(squared, 1)

            with act.Fori(0, KT // 2 - 1) as n:
                for b in range(2):
                    for hf in range(2):
                        last_square(n, b, hf)
            for hf in range(2):
                last_square(KT // 2 - 1, 0, hf)
            for hf in range(2):
                last_square(KT // 2 - 1, 1, hf)
                root(2, hf)
                act.wait_ge(rstd_made, 4 + hf)
                act.wait_ge(y_kept, START + 2 * KT - 1 + hf)
                for t in SCALED_BY_ACT[hf]:
                    A(y_nat[:, t, :], y_nat[:, t, :], ACT.Copy, scale=rstd[2][:, t:t + 1]).then_inc(y_scaled[1], 1)

        @block.vector
        def _(dve):
            dve.sem_inc(av_free, START)
            dve.sem_inc(tp_free, START)
            dve.sem_inc(hid_ready, START)
            dve.sem_inc(y_kept, START)
            V = nc.vector
            halves = [slice(0, HALF), slice(HALF, T)]

            spread = ps[:, 4:6, :].rearrange("p a b -> p (a b)")

            def ada_add(k, tile, before, first):
                ck = cols[:, COL_C + k:COL_C + k + 1]
                if first:
                    V.tensor_scalar(ada_sum[:, :], tile, ck, None, ALU.mult).then_inc(ada_used, 1)
                else:
                    dve.wait_ge(ada_used, before)
                    V.scalar_tensor_tensor(out=ada_sum[:, :], in0=tile, scalar=ck, in1=ada_sum[:, :],
                                           op0=ALU.mult, op1=ALU.add).then_inc(ada_used, 1)

            def ada_step(m, k):
                dve.wait_ge(ada_loaded[k % 2], 16 * (KT // 2 * (m - 2) + k // 2) + 16)
                if k == 0:
                    dve.wait_ge(ada_summed, m)
                ada_add(k, ada[:, k % 2, :], ADA_FIRST + KT * (m - 2) + k, k == 0)

            def mod_cols(m, order=None):
                dve.wait_ge(ada_summed, (m if order is None else order) + 1)
                V.tensor_tensor(mod[:, bass.ds(KT * m, KT)], ps[:, 6, 0:KT], cols[:, bass.ds(COL_BADA + KT * m, KT)],
                                ALU.add).then_inc(mod_made, 1)

            def add_square(n):
                dve.wait_ge(squared, n + 1)
                half = ss_b[:, halves[n % 2]]
                if n < 2:
                    ins = V.tensor_copy(half, sq_b[:, n % 2, :])
                else:
                    dve.wait_ge(sq_summed, n - 1)
                    ins = V.tensor_tensor(half, half, sq_b[:, n % 2, :], ALU.add)
                ins.then_inc(sq_summed, 1)

            def invert(which, before, tiles):
                dve.wait_ge(root_done, before + 1)
                V.reciprocal(rstd[which][:, tiles], rms[which][:, tiles]).then_inc(rstd_made, 1)
                dve.wait_ge(rstd_made, before + 1)

            def diagonals(which, diag, tiles):
                for t in tiles:
                    V.tensor_scalar(diag[:, t, :], ident[:, :], rstd[which][:, t:t + 1], None, ALU.mult).then_inc(diag_made, 1)

            def rest(which, k, tmp, h):
                dve.wait_ge(h_hi, KT * which + k + 1)
                V.scalar_tensor_tensor(out=h[1][:, k, :], in0=tmp, scalar=mod[:, 3 * KT * which + k:3 * KT * which + k + 1],
                                       in1=h[0][:, k, :].bitcast(F32), op0=ALU.add, op1=ALU.subtract).then_inc(h_ready, 1)

            for t in range(QB):
                dve.wait_ge(x_turned, 2 * t + 2)
                V.tensor_copy(xT[:, KT // 2:KT, P * t:P * t + P], ps[:, 2 * (t % 2) + 1, :].rearrange("p (k t) -> p k t", t=P)
                              ).then_inc(x_kept_dve, 1)
            dve.wait_ge(pack_turned, 1)
            V.tensor_copy(cols[:, :], ps[:, 6, 0:PACK1 + PACK2]).then_inc(cols_made, 1)
            dve.wait_ge(cols_made, 1)
            for k in range(KT):
                if k == 2:
                    invert(0, 0, slice(0, QB))
                    diagonals(0, diag_a, range(QB))
                dve.wait_ge(ada_in[k], 16)
                ada_add(k, ada_first[:, k, :], k, k == 0)
            mod_cols(1, order=0)
            dve.wait_ge(mod_made, 1)
            V.scalar_tensor_tensor(out=g_sc[0][:, :], in0=mod[:, KT:2 * KT], scalar=1.0, in1=cols[:, COL_GMIX:COL_GMIX + KT],
                                   op0=ALU.add, op1=ALU.mult).then_inc(mod_derived, 1)
            dve.wait_ge(mod_derived, 1)
            dve.wait_ge(rstd_spread, 1)
            dve.wait_ge(x_kept_act, QB)

            def x_scale(k):
                V.scalar_tensor_tensor(out=x_scaled[:, k, :], in0=xT[:, k, :], scalar=g_sc[0][:, k:k + 1], in1=spread,
                                       op0=ALU.mult, op1=ALU.mult).then_inc(normed, 1)

            def shift_add(k, before):
                dve.wait_ge(ada_in[KT + k], 16)
                ada_add(k, ada_first[:, KT + k, :], before, k == KT // 2)

            for k in range(3):
                x_scale(k)
            shift_add(4, KT)
            shift_add(5, KT + 1)
            x_scale(3)
            dve.wait_ge(ada_part, KT // 2 - 1)
            dve.wait_ge(ada_used, KT + 2)
            V.tensor_tensor(ada_sum[:, :], ada_sum[:, :], ada_first[:, KT, :], ALU.add).then_inc(ada_used, 1)
            shift_add(6, KT + 3)
            shift_add(7, KT + 4)
            for k in range(4, KT - 1):
                x_scale(k)
            mod_cols(0, order=1)
            dve.wait_ge(mod_made, 2)
            rest(0, 0, x_scaled[:, 0, :], h1)
            x_scale(KT - 1)
            for k in range(1, KT):
                rest(0, k, x_scaled[:, k, :], h1)

            fl = ps[0:HEADS, 2:4, :].rearrange("p a b -> p (a b)")
            dve.wait_ge(f_step_act, 1)
            V.tensor_scalar(f_log[:, 0:HALF], fl[:, 0:HALF], bf_col[:, 0:1], 0.0, ALU.add, ALU.min).then_inc(dense_free, 1)
            V.tensor_scalar(f_log[:, HALF:T], fl[:, HALF:T], bf_col[:, 0:1], 0.0, ALU.add, ALU.min).then_inc(dense_free, 1)
            dve.wait_ge(dense_free, FREE_F)
            dve.wait_ge(f_step_act, 3)
            V.tensor_tensor(f_log[:, :], f_log[:, :], f_abs[:, :], ALU.subtract).then_inc(f_step_dve, 1)
            dve.wait_ge(f_step_dve, 1)
            V.tensor_tensor_scan(f_cum[:, :], f_log[:, :], ones[0:HEADS, 0:1].to_broadcast([HEADS, T]), 0.0,
                                 ALU.add, ALU.mult).then_inc(f_step_dve, 1)
            dve.wait_ge(f_step_dve, 2)
            part = f_cum
            for n in range(3):
                V.tensor_copy(f_parts[:, n, :], part[:, :]).then_inc(f_step_dve, 1)
                dve.wait_ge(f_step_dve, 3 + 2 * n)
                if n == 2:
                    break
                V.tensor_tensor(f_rest[:, :], part[:, :], f_parts[:, n, :], ALU.subtract).then_inc(f_step_dve, 1)
                dve.wait_ge(f_step_dve, 4 + 2 * n)
                part = f_rest

            def outputs_lo(k):
                dve.wait_ge(o_hi_done, k + 1)
                V.tensor_tensor(o_split[1][:, k, :], mixed[:, k, :], o_split[0][:, k, :].bitcast(F32),
                                ALU.subtract).then_inc(o_ready, 1)

            def attend(G, fox, final=False):
                if not fox:
                    for k in range(4):
                        ada_step(G + 2, k)
                for hf in range(2):
                    dve.wait_ge(q_hi_done, 2 * G + hf + 1)
                    for h in range(2):
                        own = slice(DH * h, DH * h + DH)
                        for to in range(2):
                            last = V.scalar_tensor_tensor(
                                out=q_lo[h][DH * to:DH * to + DH, halves[hf]], in0=ps[own, hf, :], scalar=SCALE,
                                in1=q_hi[h][own, halves[hf]].bitcast(F32), op0=ALU.mult, op1=ALU.subtract)
                    last.then_inc(dense_free, 1)
                for hf in range(2):
                    dve.wait_ge(k_hi_done, 2 * G + hf + 1)
                    for h in range(2):
                        own, other = slice(DH * h, DH * h + DH), slice(DH * (1 - h), DH * (1 - h) + DH)
                        last = V.tensor_tensor(k_st[h][other, halves[hf]], ps[own, 2 + hf, :],
                                               k_st[h][own, halves[hf]].bitcast(F32), ALU.subtract)
                    last.then_inc(dense_free, 1)
                if not fox:
                    for k in range(4, KT):
                        ada_step(G + 2, k)

                def values_lo():
                    for idx in range(V_CHUNKS):
                        dve.wait_ge(tp_hi, TP_ITER * G + idx + 1)
                        V.tensor_tensor(v_st[:, 4 * idx:4 * idx + 4, :, 1, :],
                                        ps[:, 4 + idx, :].rearrange("p (b h d) -> p b h d", h=2, d=DH),
                                        v_st[:, 4 * idx:4 * idx + 4, :, 0, :].bitcast(F32), ALU.subtract).then_inc(tp_free, 1)
                    if not fox:
                        dve.wait_ge(f_stored, 16)
                        dve.wait_ge(x_saved, 16)

                def add_values(u):
                    h, i = divmod(u, QB)
                    own = slice(DH * h, DH * h + DH)
                    dve.wait_ge(av_folded, QB * G + u // 2 + 1)
                    q0 = P * (i - 1)
                    V.tensor_tensor(mixed[own, bass.ds(G, 1), q0:q0 + 2 * P].rearrange("p a t -> p (a t)"),
                                    ps[own, 6, 0:2 * P], fold[own, :], ALU.add).then_inc(av_free, 1)

                def weights_lo(u):
                    i = u % QB
                    q0 = P * (i % 2)
                    for n, idx in enumerate(chunks_of(u)):
                        nb = min(4, i + 1 - 4 * n)
                        dve.wait_ge(tp_hi, TP_ITER * G + idx + 1)
                        V.tensor_tensor(wT[1][:, 4 * n:4 * n + nb, q0:q0 + P],
                                        ps[:, 4 + idx % 2, 0:P * nb].rearrange("p (b q) -> p b q", q=P),
                                        wT[0][:, 4 * n:4 * n + nb, q0:q0 + P].bitcast(F32),
                                        ALU.subtract).then_inc(tp_free, 1)

                def row_max(u):
                    n = P * (u % QB + 1)
                    dve.wait_ge(scores_ready, UNITS * G + u + 1)
                    V.tensor_reduce(neg_max[:, u % 2:u % 2 + 1], scores[u % 2][:, 0:n], AX.X, ALU.max,
                                    negate=True).then_inc(max_ready, 1)

                def finish_weights(u):
                    n = P * (u % QB + 1)
                    dve.wait_ge(scores_used, START + UNITS * G + u + 1)
                    pr = prob[:, u % 2, 0:n]
                    if fox:
                        V.reciprocal(inv_sum[:, u % 2:u % 2 + 1], row_sum[:, u % 2:u % 2 + 1]).then_inc(inv_ready, 1)
                        dve.wait_ge(inv_ready, UNITS * (G - PAIRS) + u + 1)
                        V.tensor_scalar(pr, pr, inv_sum[:, u % 2:u % 2 + 1], None, ALU.mult).then_inc(probs_ready, 1)
                    else:
                        sv = surv[:, u % 2, 0:n]
                        V.tensor_tensor_scan(sv[:, ::-1], sv[:, ::-1], ones[:, 0:1].to_broadcast([P, n]), 1.0, ALU.mult,
                                             ALU.mult).then_inc(scanned, 1)
                        dve.wait_ge(scanned, UNITS * G + u + 1)
                        V.tensor_tensor(pr[:, 0:n - 1], pr[:, 0:n - 1], sv[:, 1:n], ALU.mult).then_inc(probs_ready, 1)

                for s in range(STEPS):
                    if fox and s < UNITS:
                        row_max(s)
                    if s == 1:
                        values_lo()
                    if s == 2 and not fox:
                        mod_cols(G + 2)
                    if s == STEPS - 1 and final:
                        outputs_lo(0)
                    if s >= 3 and s % 2 == 0:
                        add_values(s - 3)
                    if 2 <= s < UNITS + 2:
                        weights_lo(s - 2)
                    if s < UNITS:
                        finish_weights(s)

            with dve.Fori(0, PAIRS) as G:
                attend(G, False)
            dve.wait_ge(mod_made, N_MOD)
            for h in range(2):
                V.memset(q_f[h][:, :], -1.0).then_inc(f_ones, 1)
                V.memset(k_f[h][:, :], 1.0).then_inc(f_ones, 1)
            V.scalar_tensor_tensor(out=g_sc[1][:, :], in0=mod[:, 4 * KT:5 * KT], scalar=1.0, in1=cols[:, COL_GMLP:COL_GMLP + KT],
                                   op0=ALU.add, op1=ALU.mult).then_inc(mod_derived, 1)
            V.tensor_tensor(gt_b[:, :], mod[:, 5 * KT:6 * KT], cols[:, COL_BFF2:COL_BFF2 + KT], ALU.mult).then_inc(mod_derived, 1)
            dve.wait_ge(mod_derived, 3)
            with dve.Fori(PAIRS, 2 * PAIRS - 1) as G:
                attend(G, True)
            attend(2 * PAIRS - 1, True, final=True)

            for k in range(1, KT):
                outputs_lo(k)
            with dve.Fori(0, KT // 2) as n:
                for b in range(2):
                    for hf in range(2):
                        step = 4 * n + 2 * b + hf
                        sb, fox = (gates[:, b, m, halves[hf]] for m in range(2))
                        for m, g in enumerate((sb, fox)):
                            dve.wait_ge(gate_on, 4 * n + 2 * b + m + 1)
                            dve.wait_ge(dense_done, DONE_MERGE + 8 * n + 4 * b + 2 * m + hf + 1)
                            V.tensor_tensor(g, ps[:, 4 * b + 2 * m + hf, :], g, ALU.mult).then_inc(merge_mul, 1)
                        dve.wait_ge(merge_mul, 2 * step + 2)
                        V.tensor_tensor(sb, sb, fox, ALU.add).then_inc(merge_sum, 1)
                        dve.wait_ge(merge_hi, step + 1)
                        V.tensor_tensor(merged[1][:, bass.ds(2 * n + b, 1), halves[hf]].rearrange("p a t -> p (a t)"), sb,
                                        merged[0][:, bass.ds(2 * n + b, 1), halves[hf]].rearrange("p a t -> p (a t)").bitcast(F32),
                                        ALU.subtract).then_inc(dense_free, 1)
            def join(k, hf):
                dve.wait_ge(dense_done, DONE_WO + 2 * k + hf + 1)
                dve.wait_ge(x_back[hf], 16 * k + 16)
                V.scalar_tensor_tensor(out=res[:, k, halves[hf]], in0=ps[:, 2 * (k % 2) + hf, :],
                                       scalar=mod[:, 2 * KT + k:2 * KT + k + 1], in1=x_again[:, hf, :],
                                       op0=ALU.mult, op1=ALU.add).then_inc(dense_free, 1)

            for k in range(KT - 1):
                for hf in range(2):
                    join(k, hf)
                if k:
                    add_square(2 * k - 2)
                    add_square(2 * k - 1)
            add_square(2 * KT - 4)
            add_square(2 * KT - 3)
            for hf in range(2):
                join(KT - 1, hf)
                add_square(2 * (KT - 1) + hf)
                invert(1, 1 + hf, slice(4 * hf, 4 * hf + 4))
                diagonals(1, diag_b, range(4 * hf, 4 * hf + 4))
            dve.wait_ge(rstd_spread, 2)
            for k in range(KT):
                if k >= 2:
                    dve.wait_ge(h_ready, KT + k - 1)
                V.scalar_tensor_tensor(out=norm_b[:, k % 2, :], in0=res[:, k, :], scalar=g_sc[1][:, k:k + 1],
                                       in1=spread, op0=ALU.mult, op1=ALU.mult).then_inc(normed, 1)
                if k:
                    rest(1, k - 1, norm_b[:, (k - 1) % 2, :], h2)
            rest(1, KT - 1, norm_b[:, (KT - 1) % 2, :], h2)
            dve.wait_ge(act_free, KT)
            def hidden(ch):
                with dve.Fori(0, KT) as n:
                    for hf in range(2):
                        step = 2 * KT * ch + 2 * n + hf
                        dve.wait_ge(act_free, KT + step + 1)
                        V.tensor_tensor(relu_sq[:, hf, :], relu[:, hf, :], relu[:, hf, :], ALU.mult).then_inc(relu_squared, 1)
                        dve.wait_ge(relu_squared, step + 1)
                        dve.wait_ge(hid_hi, step + 1)
                        V.tensor_tensor(hid[1][:, bass.ds(n, 1), halves[hf]].rearrange("p a t -> p (a t)"), relu_sq[:, hf, :],
                                        hid[0][:, bass.ds(n, 1), halves[hf]].rearrange("p a t -> p (a t)").bitcast(F32),
                                        ALU.subtract).then_inc(hid_ready, 1)

            def residual(ch, n, b, out_tile=None, hfs=(0, 1)):
                for hf in hfs:
                    step = 2 * KT * ch + 4 * n + 2 * b + hf
                    dve.wait_ge(dense_done, DONE_FF + 4 * KT * ch + 2 * KT + 4 * n + 2 * b + hf + 1)
                    dve.wait_ge(dense_free, FREE_FF - 2 * KT + step + 1)
                    tile = res[:, bass.ds(2 * n + b, 1), halves[hf]].rearrange("p a t -> p (a t)")
                    V.scalar_tensor_tensor(out=tile if out_tile is None else out_tile[:, halves[hf]], in0=ps[:, 2 * b + hf, :],
                                           scalar=mod[:, bass.ds(5 * KT + 2 * n + b, 1)], in1=tile,
                                           op0=ALU.mult, op1=ALU.add).then_inc(dense_free, 1)

            with dve.Fori(0, FF_CHUNKS - 1) as ch:
                hidden(ch)
                with dve.Fori(0, KT // 2) as n:
                    for b in range(2):
                        residual(ch, n, b)
            hidden(FF_CHUNKS - 1)
            dve.wait_ge(gain_loaded, 16)

            def sum_squares(tile, first=False, hfs=(0, 1)):
                for hf in hfs:
                    n = 2 * tile + hf
                    dve.wait_ge(squared, 2 * KT + n + 1)
                    dve.wait_ge(sq_summed, 2 * KT + n - 1)
                    half = ss_b[:, halves[hf]]
                    if first:
                        V.tensor_copy(half, sq_b[:, hf, :]).then_inc(sq_summed, 1)
                    else:
                        V.tensor_tensor(half, half, sq_b[:, hf, :], ALU.add).then_inc(sq_summed, 1)

            def keep(tile, b, hfs=(0, 1)):
                for hf in hfs:
                    dve.wait_ge(y_turned, 2 * tile + hf + 1)
                    V.tensor_tensor(y_nat[:, 4 * hf:4 * hf + 4, bass.ds(P * tile, P)],
                                    ps[:, 4 + 2 * b + hf, :].rearrange("p (t d) -> p t d", d=P),
                                    gain_row[:, bass.ds(P * tile, P)].unsqueeze(1).broadcast_to([P, 4, P]),
                                    ALU.mult).then_inc(y_kept, 1)

            def last_pair(n, first):
                if not first:
                    keep(2 * n - 1, 1)
                residual(FF_CHUNKS - 1, n, 0, y_st[:, 0, :])
                sum_squares(2 * n, first)
                keep(2 * n, 0)
                residual(FF_CHUNKS - 1, n, 1, y_st[:, 1, :])
                sum_squares(2 * n + 1)

            last_pair(0, True)
            with dve.Fori(1, KT // 2 - 1) as n:
                last_pair(n, False)
            n = KT // 2 - 1
            keep(2 * n - 1, 1)
            residual(FF_CHUNKS - 1, n, 0, y_st[:, 0, :])
            sum_squares(2 * n)
            keep(2 * n, 0)
            for hf in range(2):
                residual(FF_CHUNKS - 1, n, 1, y_st[:, 1, :], hfs=(hf,))
                sum_squares(2 * n + 1, hfs=(hf,))
                keep(KT - 1, 1, hfs=(hf,))
                invert(2, 3 + hf, slice(4 * hf, 4 * hf + 4))
                dve.wait_ge(y_kept, START + 2 * KT - 1 + hf)
                for t in range(4 * hf, 4 * hf + 4):
                    if t not in SCALED_BY_ACT[hf]:
                        V.tensor_scalar(y_nat[:, t, :], y_nat[:, t, :], rstd[2][:, t:t + 1], None, ALU.mult
                                        ).then_inc(y_scaled[0], 1)


_INS = ["x", "c", "w_ada", "b_ada", "g_mix", "w_in", "b_f", "w_gate", "b_gate", "w_out_sb", "w_out_fox",
        "w_o", "g_mlp", "w_ff1", "b_ff1", "w_ff2", "b_ff2", "g_final"]


def kernel(**inputs):
    import numpy as np
    import concourse.bacc as bacc
    from concourse.bass_utils import run_bass_kernel_spmd

    nc = bacc.Bacc("TRN2", target_bir_lowering=False, num_devices=1)
    arrays, args = {}, []
    for name in _INS:
        a = np.ascontiguousarray(inputs[name])
        arrays[f"in_{name}"] = a
        args.append(nc.dram_tensor(f"in_{name}", a.shape, mybir.dt.from_np(a.dtype), kind="ExternalInput").ap())
    shape = inputs["x"].shape
    args.append(nc.dram_tensor("out_0", shape, F32, kind="ExternalOutput").ap())
    build_block(nc, *args)
    r = run_bass_kernel_spmd(nc, [arrays], core_ids=[0])
    return r.results[0]["out_0"]
```
